# Optimizing a Trainium2 kernel written in Bass

```python
import math
import jax, jax.numpy as jnp
from jax import lax
import numpy as np
import jax
import jax.numpy as jnp

D_MODEL = 1024
BATCH = 1
SEQ = 256
DEPTH = 2

N_HEADS = 16
HEAD_DIM = D_MODEL // N_HEADS
CONV_WIDTH = 31
D_FF = ((8 * D_MODEL // 3) + 127) // 128 * 128
N_EXPERTS = 8
TOP_K = 2
Q_BLOCK = 128
EPS = 1e-6
N_A_LAYERS = (DEPTH + 1) // 2
N_B_LAYERS = DEPTH - N_A_LAYERS
N_DENSE = (DEPTH + 1) // 2
N_MOE = DEPTH // 2
FORGET_BIAS_MEAN = 2.0


def rms_norm(x, g):
    xf = x.astype(jnp.float32)
    y = xf * lax.rsqrt(jnp.mean(xf * xf, axis=-1, keepdims=True) + EPS)
    return (y * g.astype(jnp.float32)).astype(x.dtype)

def layer_norm(x, g, b):
    xf = x.astype(jnp.float32)
    mu = jnp.mean(xf, axis=-1, keepdims=True)
    var = jnp.mean(jnp.square(xf - mu), axis=-1, keepdims=True)
    y = (xf - mu) * lax.rsqrt(var + EPS)
    return (y * g.astype(jnp.float32) + b.astype(jnp.float32)).astype(x.dtype)

def conformer_conv(h, w_in, b_in, w_dw, b_dw, ln_g, ln_b, w_out, b_out):
    u = h @ w_in + b_in
    a, gate = jnp.split(u, 2, axis=-1)
    u = a * jax.nn.sigmoid(gate)
    u = lax.conv_general_dilated(
        u, w_dw[:, None, :].astype(u.dtype),
        window_strides=(1,), padding=[(CONV_WIDTH - 1, 0)],
        dimension_numbers=("NWC", "WIO", "NWC"),
        feature_group_count=D_MODEL) + b_dw
    u = layer_norm(u, ln_g, ln_b)
    u = jax.nn.silu(u)
    return u @ w_out + b_out

def swiglu(h, w_gate, w_up, w_down):
    return (jax.nn.silu(h @ w_gate) * (h @ w_up)) @ w_down

def moe_swiglu(h, router_w, router_b, w_gate, w_up, w_down):
    logits = (h @ router_w + router_b).astype(jnp.float32)
    top_vals, top_idx = lax.top_k(logits, TOP_K)
    top_p = jax.nn.softmax(top_vals, axis=-1)
    gates = jnp.sum(jax.nn.one_hot(top_idx, N_EXPERTS, dtype=jnp.float32) * top_p[..., None], axis=-2)
    gates = gates.astype(h.dtype)
    out = jnp.zeros_like(h)
    for e in range(N_EXPERTS):
        out = out + gates[..., e:e + 1] * swiglu(h, w_gate[e], w_up[e], w_down[e])
    return out

def shared_kv(x, kv_norm, w_kvf, b_f):
    bsz, seq, _ = x.shape
    hn = rms_norm(x, kv_norm)
    proj = hn @ w_kvf
    k = proj[..., :D_MODEL].reshape(bsz, seq, N_HEADS, HEAD_DIM)
    v = proj[..., D_MODEL:2 * D_MODEL].reshape(bsz, seq, N_HEADS, HEAD_DIM)
    f_logit = proj[..., 2 * D_MODEL:].astype(jnp.float32) + b_f.astype(jnp.float32)
    logf_cum = jnp.cumsum(jax.nn.log_sigmoid(f_logit), axis=1)
    return k, v, jnp.transpose(logf_cum, (0, 2, 1))

def forgetting_attention(q, k, v, logf_cum):
    seq = q.shape[1]
    scale = HEAD_DIM ** -0.5
    qf = q.astype(jnp.float32)
    kf = k.astype(jnp.float32)
    outs = []
    for blk in range(seq // Q_BLOCK):
        q0 = blk * Q_BLOCK
        q1 = q0 + Q_BLOCK
        s = jnp.einsum("bqhd,bkhd->bhqk", qf[:, q0:q1], kf[:, :q1]) * scale
        s = s + logf_cum[:, :, q0:q1, None] - logf_cum[:, :, None, :q1]
        mask = (q0 + jnp.arange(Q_BLOCK))[:, None] >= jnp.arange(q1)[None, :]
        s = jnp.where(mask, s, -jnp.inf)
        p = jax.nn.softmax(s, axis=-1).astype(v.dtype)
        outs.append(jnp.einsum("bhqk,bkhd->bqhd", p, v[:, :q1]))
    return jnp.concatenate(outs, axis=1)

def first_inputs(seed: int = 0) -> dict:
    key = jax.random.key(seed)
    ks = jax.random.split(key, 32)
    f32 = jnp.float32

    def w(k, shape, fan_in):
        return jax.random.normal(k, shape, f32) * (fan_in ** -0.5)

    def gain(k, shape):
        return 1.0 + 0.02 * jax.random.normal(k, shape, f32)

    def bias(k, shape, scale=0.02):
        return scale * jax.random.normal(k, shape, f32)

    D = D_MODEL
    return {
        "x": jax.random.normal(ks[0], (BATCH, SEQ, D), f32),
        "mix_norm": gain(ks[1], (DEPTH, D)),
        "ffn_norm": gain(ks[2], (DEPTH, D)),
        "conv_w_in": w(ks[3], (N_A_LAYERS, D, 2 * D), D),
        "conv_b_in": bias(ks[4], (N_A_LAYERS, 2 * D)),
        "conv_w_dw": w(ks[5], (N_A_LAYERS, CONV_WIDTH, D), CONV_WIDTH),
        "conv_b_dw": bias(ks[6], (N_A_LAYERS, D)),
        "conv_ln_g": gain(ks[7], (N_A_LAYERS, D)),
        "conv_ln_b": bias(ks[8], (N_A_LAYERS, D)),
        "conv_w_out": w(ks[9], (N_A_LAYERS, D, D), D),
        "conv_b_out": bias(ks[10], (N_A_LAYERS, D)),
        "kv_norm": gain(ks[11], (D,)),
        "w_kvf": w(ks[12], (D, 2 * D + N_HEADS), D),
        "b_f": FORGET_BIAS_MEAN + 0.5 * jax.random.normal(ks[13], (N_HEADS,), f32),
        "w_q": w(ks[14], (N_B_LAYERS, D, D), D),
        "w_o": w(ks[15], (N_B_LAYERS, D, D), D),
        "ffn_w_gate": w(ks[16], (N_DENSE, D, D_FF), D),
        "ffn_w_up": w(ks[17], (N_DENSE, D, D_FF), D),
        "ffn_w_down": w(ks[18], (N_DENSE, D_FF, D), D_FF),
        "router_w": w(ks[19], (N_MOE, D, N_EXPERTS), D),
        "router_b": bias(ks[20], (N_MOE, N_EXPERTS), 0.01),
        "moe_w_gate": w(ks[21], (N_MOE, N_EXPERTS, D, D_FF), D),
        "moe_w_up": w(ks[22], (N_MOE, N_EXPERTS, D, D_FF), D),
        "moe_w_down": w(ks[23], (N_MOE, N_EXPERTS, D_FF, D), D_FF),
        "final_norm": gain(ks[24], (D,)),
    }

def first_block(x, mix_norm, ffn_norm, conv_w_in, conv_b_in, conv_w_dw, conv_b_dw, conv_ln_g, conv_ln_b,
              conv_w_out, conv_b_out, kv_norm, w_kvf, b_f, w_q, w_o, ffn_w_gate, ffn_w_up, ffn_w_down,
              router_w, router_b, moe_w_gate, moe_w_up, moe_w_down, final_norm):
    bsz, seq, _ = x.shape
    a_i = b_i = d_i = m_i = 0
    k = v = logf_cum = None
    for layer in range(DEPTH):
        h = rms_norm(x, mix_norm[layer])
        if layer < N_A_LAYERS:
            x = x + conformer_conv(h, conv_w_in[a_i], conv_b_in[a_i], conv_w_dw[a_i], conv_b_dw[a_i],
                                   conv_ln_g[a_i], conv_ln_b[a_i], conv_w_out[a_i], conv_b_out[a_i])
            a_i += 1
        else:
            if k is None:
                k, v, logf_cum = shared_kv(x, kv_norm, w_kvf, b_f)
            q = (h @ w_q[b_i]).reshape(bsz, seq, N_HEADS, HEAD_DIM)
            o = forgetting_attention(q, k, v, logf_cum).reshape(bsz, seq, D_MODEL)
            x = x + o @ w_o[b_i]
            b_i += 1
        h = rms_norm(x, ffn_norm[layer])
        if layer % 2 == 0:
            x = x + swiglu(h, ffn_w_gate[d_i], ffn_w_up[d_i], ffn_w_down[d_i])
            d_i += 1
        else:
            x = x + moe_swiglu(h, router_w[m_i], router_b[m_i], moe_w_gate[m_i], moe_w_up[m_i], moe_w_down[m_i])
            m_i += 1
    return rms_norm(x, final_norm)


N_MIXERS = 2
N_POOL_LAYERS = (DEPTH + 1) // 2
N_ATTN_LAYERS = DEPTH // 2

POOL_WINDOWS = (2, 4, 8, 16)
N_POOL_GROUPS = len(POOL_WINDOWS)
POOL_GC = D_MODEL // N_POOL_GROUPS

HEAD_DIM_2 = 64
N_HEADS_2 = D_MODEL // HEAD_DIM_2
N_KV_HEADS = 4
N_GROUPS = N_HEADS_2 // N_KV_HEADS
WINDOW = 128
BLOCK = 128
QKV_DIM = (N_HEADS_2 + 2 * N_KV_HEADS) * HEAD_DIM_2

D_FF_2 = 2816
CONV_W = 3

RMS_EPS = 1e-6


def rms_norm_2(x, g):
    xf = x.astype(jnp.float32)
    y = xf * lax.rsqrt(jnp.mean(xf * xf, axis=-1, keepdims=True) + RMS_EPS)
    return (y * g.astype(jnp.float32)).astype(x.dtype)

def alibi_slopes(n_heads):
    h = jnp.arange(1, n_heads + 1, dtype=jnp.float32)
    return jnp.exp2(-8.0 / n_heads * h)

def pool_mixer(h, w, b, scale):
    B, S, D = h.shape
    hf = h.astype(jnp.float32)
    csum = jnp.cumsum(hf, axis=1)
    t1 = jnp.arange(1, S + 1)
    outs = []
    for gi, win in enumerate(POOL_WINDOWS):
        sl = slice(gi * POOL_GC, (gi + 1) * POOL_GC)
        c = csum[..., sl]
        lo = jnp.pad(c, ((0, 0), (win, 0), (0, 0)))[:, :S]
        count = jnp.minimum(t1, win).astype(jnp.float32)
        mean = (c - lo) / count[None, :, None]
        outs.append(mean - hf[..., sl])
    p = jnp.stack(outs, axis=2).astype(h.dtype)
    y = jnp.einsum('bsgc,gcd->bsgd', p, w) + b
    return y.reshape(B, S, D) * scale

def swa_sink_attention(h, w_qkv, b_qkv, sinks, w_o):
    B, S, _ = h.shape
    nb = S // BLOCK
    qkv = h @ w_qkv + b_qkv
    q = qkv[..., :N_HEADS_2 * HEAD_DIM_2].reshape(B, nb, BLOCK, N_KV_HEADS, N_GROUPS, HEAD_DIM_2)
    k = qkv[..., N_HEADS_2 * HEAD_DIM_2:(N_HEADS_2 + N_KV_HEADS) * HEAD_DIM_2].reshape(B, S, N_KV_HEADS, HEAD_DIM_2)
    v = qkv[..., (N_HEADS_2 + N_KV_HEADS) * HEAD_DIM_2:].reshape(B, S, N_KV_HEADS, HEAD_DIM_2)

    def band(t):
        tp = jnp.pad(t, ((0, 0), (BLOCK, 0), (0, 0), (0, 0)))[:, :S]
        prev = tp.reshape(B, nb, BLOCK, N_KV_HEADS, HEAD_DIM_2)
        cur = t.reshape(B, nb, BLOCK, N_KV_HEADS, HEAD_DIM_2)
        return jnp.concatenate([prev, cur], axis=2)

    kb, vb = band(k), band(v)
    scores = jnp.einsum('bnqkgd,bnskd->bnkgqs', q, kb).astype(jnp.float32) * (HEAD_DIM_2 ** -0.5)

    qi = jnp.arange(BLOCK)[:, None]
    kj = jnp.arange(2 * BLOCK)[None, :]
    dist = qi + BLOCK - kj
    key_pos = jnp.arange(nb)[:, None] * BLOCK - BLOCK + jnp.arange(2 * BLOCK)[None, :]
    mask = ((dist >= 0) & (dist < WINDOW))[None] & (key_pos >= 0)[:, None, :]

    slopes = alibi_slopes(N_HEADS_2).reshape(N_KV_HEADS, N_GROUPS)
    bias = -slopes[:, :, None, None] * dist.astype(jnp.float32)[None, None]
    scores = jnp.where(mask[None, :, None, None], scores + bias, -jnp.inf)

    sink = sinks.astype(jnp.float32).reshape(N_KV_HEADS, N_GROUPS)[None, None, :, :, None, None]
    m = jnp.maximum(jnp.max(scores, axis=-1, keepdims=True), sink)
    p = jnp.exp(scores - m)
    denom = jnp.sum(p, axis=-1, keepdims=True) + jnp.exp(sink - m)
    probs = (p / denom).astype(v.dtype)
    o = jnp.einsum('bnkgqs,bnskd->bnqkgd', probs, vb).reshape(B, S, N_HEADS_2 * HEAD_DIM_2)
    return o @ w_o

def conv_glu_ffn(h, w_in, conv_w, conv_b, w_out):
    u = h @ w_in
    c = lax.conv_general_dilated(
        u, conv_w[:, None, :].astype(u.dtype), window_strides=(1,),
        padding=[(CONV_W - 1, 0)], dimension_numbers=('NWC', 'WIO', 'NWC'),
        feature_group_count=2 * D_FF_2) + conv_b
    a, g = c[..., :D_FF_2], c[..., D_FF_2:]
    return (a * jax.nn.silu(g)) @ w_out

def second_inputs(seed: int = 0) -> dict:
    key = jax.random.key(seed)
    ks = jax.random.split(key, 16)
    f32 = jnp.float32
    nrm = lambda k, shape, s: jax.random.normal(k, shape, f32) * s
    return {
        "x": nrm(ks[0], (BATCH, SEQ, D_MODEL), 1.0),
        "pool_w": nrm(ks[1], (N_POOL_LAYERS, N_POOL_GROUPS, POOL_GC, POOL_GC), POOL_GC ** -0.5),
        "pool_b": nrm(ks[2], (N_POOL_LAYERS, N_POOL_GROUPS, POOL_GC), 0.02),
        "pool_scale": 1.0 + nrm(ks[3], (N_POOL_LAYERS, D_MODEL), 0.05),
        "attn_w_qkv": nrm(ks[4], (N_ATTN_LAYERS, D_MODEL, QKV_DIM), D_MODEL ** -0.5),
        "attn_b_qkv": nrm(ks[5], (N_ATTN_LAYERS, QKV_DIM), 0.02),
        "attn_sinks": nrm(ks[6], (N_ATTN_LAYERS, N_HEADS_2), 0.5),
        "attn_w_o": nrm(ks[7], (N_ATTN_LAYERS, N_HEADS_2 * HEAD_DIM_2, D_MODEL), (N_HEADS_2 * HEAD_DIM_2) ** -0.5),
        "norm_mix": 1.0 + nrm(ks[8], (DEPTH, D_MODEL), 0.05),
        "norm_ffn": 1.0 + nrm(ks[9], (DEPTH, D_MODEL), 0.05),
        "ffn_w_in": nrm(ks[10], (DEPTH, D_MODEL, 2 * D_FF_2), D_MODEL ** -0.5),
        "ffn_conv_w": nrm(ks[11], (DEPTH, CONV_W, 2 * D_FF_2), CONV_W ** -0.5),
        "ffn_conv_b": nrm(ks[12], (DEPTH, 2 * D_FF_2), 0.02),
        "ffn_w_out": nrm(ks[13], (DEPTH, D_FF_2, D_MODEL), D_FF_2 ** -0.5),
        "norm_f": 1.0 + nrm(ks[14], (D_MODEL,), 0.05),
    }

def second_block(x, pool_w, pool_b, pool_scale, attn_w_qkv, attn_b_qkv, attn_sinks, attn_w_o,
              norm_mix, norm_ffn, ffn_w_in, ffn_conv_w, ffn_conv_b, ffn_w_out, norm_f):
    h = x
    for i in range(DEPTH):
        hn = rms_norm_2(h, norm_mix[i])
        j = i // N_MIXERS
        if i % N_MIXERS == 0:
            mix = pool_mixer(hn, pool_w[j], pool_b[j], pool_scale[j])
        else:
            mix = swa_sink_attention(hn, attn_w_qkv[j], attn_b_qkv[j], attn_sinks[j], attn_w_o[j])
        h = h + mix
        hn = rms_norm_2(h, norm_ffn[i])
        h = h + conv_glu_ffn(hn, ffn_w_in[i], ffn_conv_w[i], ffn_conv_b[i], ffn_w_out[i])
    return rms_norm_2(h, norm_f)


def setup_inputs(seed=0):
    out = dict(first_inputs(seed))
    for name, value in second_inputs(seed + 1).items():
        if name != "x":
            out[name + "_2"] = value
    return out


def reference(
    x, mix_norm, ffn_norm, conv_w_in, conv_b_in, conv_w_dw, conv_b_dw, conv_ln_g, conv_ln_b,
    conv_w_out, conv_b_out, kv_norm, w_kvf, b_f, w_q, w_o, ffn_w_gate, ffn_w_up, ffn_w_down,
    router_w, router_b, moe_w_gate, moe_w_up, moe_w_down, final_norm, pool_w_2, pool_b_2,
    pool_scale_2, attn_w_qkv_2, attn_b_qkv_2, attn_sinks_2, attn_w_o_2, norm_mix_2, norm_ffn_2,
    ffn_w_in_2, ffn_conv_w_2, ffn_conv_b_2, ffn_w_out_2, norm_f_2,
):
    x = first_block(
        x, mix_norm, ffn_norm, conv_w_in, conv_b_in, conv_w_dw, conv_b_dw, conv_ln_g, conv_ln_b,
        conv_w_out, conv_b_out, kv_norm, w_kvf, b_f, w_q, w_o, ffn_w_gate, ffn_w_up, ffn_w_down,
        router_w, router_b, moe_w_gate, moe_w_up, moe_w_down, final_norm,
    )
    return second_block(
        x, pool_w_2, pool_b_2, pool_scale_2, attn_w_qkv_2, attn_b_qkv_2, attn_sinks_2,
        attn_w_o_2, norm_mix_2, norm_ffn_2, ffn_w_in_2, ffn_conv_w_2, ffn_conv_b_2, ffn_w_out_2,
        norm_f_2,
    )


_drawn_inputs = setup_inputs


def setup_inputs(seed=0):
    import zlib

    import numpy as np

    out = dict(_drawn_inputs(seed))
    spreads = {}
    factors = {'pool_b_2': 2.817, 'attn_b_qkv_2': 4.136, 'ffn_conv_b_2': 3.291}
    for name, (base, spread) in spreads.items():
        noise = np.random.default_rng([zlib.crc32(name.encode()), seed]).standard_normal(out[name].shape)
        drawn = base * np.exp(spread * noise) if base else spread * noise
        out[name] = jnp.asarray(drawn.astype(out[name].dtype))
    for name, factor in factors.items():
        out[name] = (out[name] * factor).astype(out[name].dtype)
    return out
```

```python
import math
from contextlib import ExitStack

import concourse.bass as bass
from concourse import mybir

F32 = mybir.dt.float32
F32R = mybir.dt.float32r
U32 = mybir.dt.uint32
I32 = mybir.dt.int32
ALU = mybir.AluOpType
ACT = mybir.ActivationFunctionType
AX_X = mybir.AxisListType.X

P = 128
D = 1024
S = 256
T = S // P
KC = D // P
F = 2816
STEP = 256
NSTEP = F // STEP
DOUBLE = (NSTEP - 1) // 2
E = 8
H = 16
HD = 64
KVH = 4
TAPS = 31
PAD = TAPS - 1
CTAPS = 3
WINDOWS = (2, 4, 8, 16)
MAXW = max(WINDOWS)
EPS = 1e-6
NEG = -1e30
RING = 6
WORK = 9216
UNIT = 2048
FFN_UNITS = 3 * NSTEP

U_CONV_IN = 0
U_CONV_OUT = U_CONV_IN + 8
U_FFN1 = U_CONV_OUT + 4
U_K = U_FFN1 + FFN_UNITS
U_V = U_K + 4
U_Q = U_V + 4
U_WO = U_Q + 4
U_MOE = U_WO + 4
U_POOL = U_MOE + E * FFN_UNITS
U_FFN2A = U_POOL + 1
U_Q2 = U_FFN2A + FFN_UNITS
U_KV2 = U_Q2 + 4
U_WO2 = U_KV2 + 2
U_FFN2B = U_WO2 + 4
U_END = U_FFN2B + FFN_UNITS

VECTORS = [("mix_norm", 16), ("ffn_norm", 16), ("kv_norm", 8), ("conv_b_in", 16), ("conv_w_dw", 8 * TAPS),
           ("conv_b_dw", 8), ("conv_ln_g", 8), ("conv_ln_b", 8), ("norm_mix_2", 16), ("norm_ffn_2", 16),
           ("attn_b_qkv_2", 12), ("ffn_conv_w_2", 2 * CTAPS * 44), ("ffn_conv_b_2", 2 * 44)]
COL, _n = {}, 0
for _name, _rows in VECTORS:
    COL[_name] = _n
    _n += _rows
NCOL = _n
NBLK = -(-NCOL // P)


def lin(base, d, per):
    return base if d is None else d * per + base


def build(nc, a, out):
    with ExitStack() as ctx:
        def sb(name, shape, dt=F32):
            return ctx.enter_context(nc.sbuf_tensor(name, shape, dt))

        def sem(name):
            return ctx.enter_context(nc.semaphore(name))

        ps = ctx.enter_context(nc.psum_tensor("ps", [P, 8, 512], F32))
        work_at = -(-nc.sbuf_base // 32) * 32
        work = sb("work", [P, WORK])
        assert nc.sbuf_base == work_at + 4 * WORK
        raw = sb("raw", [P, RING, UNIT])
        whi = sb("whi", [P, RING, UNIT], F32R)
        wlo = sb("wlo", [P, RING, UNIT], F32R)
        X = sb("X", [P, T, D])
        xh = sb("xh", [P, KC, S], F32R)
        xl = sb("xl", [P, KC, S], F32R)
        V = sb("V", [P, NCOL])
        bc = sb("bc", [P, 2, D])
        ident = sb("ident", [P, P])
        ones = sb("ones", [P, P])
        tri = sb("tri", [P, S])
        order = tri
        mask = sb("mask", [P, S])
        dist = mask
        ind = sb("ind", [P, 2, 16])
        rows = sb("rows", [P, 2])
        dsel = sb("dsel", [P, 8])
        iota8 = sb("iota8", [P, E])
        wf_raw = sb("wf_raw", [P, KC, H])
        wf = sb("wf", [P, 2, KC, H], F32R)
        wr_raw = sb("wr_raw", [P, KC, E])
        wr = sb("wr", [P, 2, KC, E], F32R)
        bf = sb("bf", [P, H])
        rb = sb("rb", [P, E])
        sink = sb("sink", [P, H])
        sink8 = sb("sink8", [P, H])
        bv2 = bc[:, 1, 0:256]
        st = sb("st", [P, 64])
        fz = sb("fz", [P, 4, T, H])
        gate = sb("gate", [P, T, E])
        gl = sb("gl", [P, 4, T, E])
        gi = sb("gi", [P, T, 8], U32)
        rmax = sb("rmax", [P, 8, 4])
        nmax = sb("nmax", [P, 8, 4])
        rsum = sb("rsum", [P, 8, 4])
        esink = sb("esink", [P, 8, 4])
        rinv = sb("rinv", [P, 8, 4])

        def wk(at, *shape):
            n = math.prod(shape)
            v = work[:, at:at + n]
            if len(shape) == 2:
                return v.rearrange("p (a b) -> p a b", b=shape[1])
            if len(shape) == 3:
                return v.rearrange("p (a b c) -> p a b c", b=shape[1], c=shape[2])
            return v

        def wkr(name, at, *shape):
            return nc.alloc_sbuf_tensor_at(name, [P, *shape], F32R, offset=work_at + 4 * at)

        Y = {"low": wk(0, T, D), "high": wk(4096, T, D)}
        junk = {"low": wk(2048, D), "high": wk(6144, D)}
        U = wk(0, KC, PAD + S)
        SGc = wk(2304, 2, S)
        C = wk(3072, KC, S)
        MU = wk(5120, S)
        RS = wk(5376, S)
        VAR = wk(7680, S)
        Z = wk(5632, KC, S)
        stage = wk(8192, NBLK, P)
        SG = wk(0, 2, S)
        Ht = wk(512, 2, S)
        hh = wkr("hh", 1024, 2, 2, S)
        hl = wkr("hl", 2048, 2, 2, S)
        U2 = wk(3072, 4, 2 + S)
        C2 = wk(4104, 4, S)
        hnh = wkr("hnh", 0, KC, S)
        hnl = wkr("hnl", 2048, KC, S)
        qT = wk(0, KC, S)
        SC = wk(2048, 4, S)
        PT = wk(3072, 2, 4, P)
        kT = wk(4096, KC, S)
        vt = wk(6144, T, D)
        Mq = wk(8192, S)
        Mk = wk(8448, S)
        MH = wk(8704, 2, 2, P)
        Lc = wk(8704, T, P)
        kT2 = wk(4096, KVH, S)
        vt2 = wk(6144, T, 256)
        count = wk(2048, 4, S)
        HF = wk(3072, KC, MAXW + S)
        SA = wk(5248, 2, MAXW + S)
        SB = wk(5792, 2, MAXW + S)
        PO = wk(6400, KC, S)

        x_in = sem("x_in")
        vec_in = sem("vec_in")
        small_in = sem("small_in")
        bc_in = sem("bc_in")
        bc_free = sem("bc_free")
        out_done = sem("out_done")
        ident_ready = sem("ident_ready")
        consts_ready = sem("consts_ready")
        pool_chain = sem("pool_chain")
        dve_chain = sem("dve_chain")
        act_chain = sem("act_chain")
        vec_ps = sem("vec_ps")
        vec_ready = sem("vec_ready")
        raw_in = [sem(f"raw_in{s}") for s in range(RING)]
        hi_done = sem("hi_done")
        lo_done = sem("lo_done")
        unit_used = sem("unit_used")
        y_ready = sem("y_ready")
        xt_ps = sem("xt_ps")
        xt_hi = sem("xt_hi")
        xt_lo = sem("xt_lo")
        acc_ps = sem("acc_ps")
        acc_free = sem("acc_free")
        cin_ps = sem("cin_ps")
        cin_sig = sem("cin_sig")
        cin_mul = sem("cin_mul")
        tap_done = sem("tap_done")
        conv_done = sem("conv_done")
        stat_ps = sem("stat_ps")
        centered = sem("centered")
        squared = sem("squared")
        scaled = sem("scaled")
        z_ready = sem("z_ready")
        kinds = {}
        for kind in ("glu", "cglu"):
            kinds[kind] = {n: sem(f"{kind}_{n}") for n in ("ps", "copy", "conv", "tap", "silu", "mul", "hi", "lo")}
        small_hi = sem("small_hi")
        small_lo = sem("small_lo")
        qk_ps = sem("qk_ps")
        qk_out = sem("qk_out")
        f_ps = sem("f_ps")
        f_z = sem("f_z")
        f_ln = sem("f_ln")
        cum_in = sem("cum_in")
        cum_ps = sem("cum_ps")
        cum_ready = sem("cum_ready")
        mh_ready = sem("mh_ready")
        sc_ps = sem("sc_ps")
        sc_max = sem("sc_max")
        sc_exp = sem("sc_exp")
        sc_norm = sem("sc_norm")
        pt_ps = sem("pt_ps")
        pt_a = sem("pt_a")
        pt_v = sem("pt_v")
        o_ps = sem("o_ps")
        o_hi = sem("o_hi")
        o_lo = sem("o_lo")
        r_ps = sem("r_ps")
        r_top = sem("r_top")
        r_exp = sem("r_exp")
        pads = sem("pads")
        z_lo = sem("z_lo")
        v2_ready = sem("v2_ready")
        hf_ready = sem("hf_ready")
        po_ready = sem("po_ready")

        block = ctx.enter_context(nc.Block())

        BC = [(0, a["conv_b_out"]), (1, a["final_norm"]), (0, a["pool_b_2"]), (1, a["pool_scale_2"]), (0, a["norm_f_2"])]

        def spread(v, n):
            flat = v
            while len(flat.shape) > 1:
                names = "abcd"[:len(flat.shape)]
                flat = flat.rearrange(f"{' '.join(names)} -> ({' '.join(names)})")
            return flat[0:n].unsqueeze(0).to_broadcast([P, n])

        def vector_rows():
            pieces = []
            for name, nrow in VECTORS:
                v = a[name]
                names = "abcd"[:len(v.shape)]
                v = v.rearrange(f"{' '.join(names)} -> ({' '.join(names)})").rearrange("(r c) -> r c", c=P)
                r = 0
                while r < nrow:
                    at = COL[name] + r
                    m = min(nrow - r, P - at % P)
                    pieces.append((at, v[r:r + m, :], m))
                    r += m
            return pieces

        @block.sync
        def _(sp):
            def kmaj(w, k0, nk, c0, nc_):
                return w[k0 * P:(k0 + nk) * P, c0:c0 + nc_].rearrange("(k p) c -> p k c", p=P)

            def load(u, parts, d=None):
                s = u % RING
                if d is not None or u >= RING:
                    sp.wait_ge(lo_done, lin(u - RING + 1, d, 6))
                for dst, src in parts:
                    sp.dma_start(dst, src).then_inc(raw_in[s], 16)

            def tall(u, w, k0, c0=0, d=None):
                s = u % RING
                load(u, [(raw[:, s, i * D:(i + 1) * D], w[(k0 + i) * P:(k0 + i + 1) * P, c0:c0 + D]) for i in range(2)], d)

            def pair(u, wa, ca, wb, cb, k0, d=None):
                v = raw[:, u % RING, :].rearrange("p (k h c) -> p k h c", k=4, h=2)
                load(u, [(v[:, :, h, :], w[k0 * P:(k0 + 4) * P, c].rearrange("(k p) c -> p k c", p=P))
                         for h, w, c in ((0, wa, ca), (1, wb, cb))], d)

            def ffn(u, wg, wu, wd, shift=0, up_at=0, outer=None):
                def gate_up(u, s, j, d):
                    col = lin(s * STEP, j, 2 * STEP)
                    colu = lin(s * STEP + up_at, j, 2 * STEP)
                    for kh in range(2):
                        pair(u + kh, wg, bass.ds(col, STEP), wu, bass.ds(colu, STEP), 4 * kh, d)

                def down(u, s, j, d):
                    r = u % RING
                    load(u, [(raw[:, r, i * D:(i + 1) * D], wd[bass.ds(lin((2 * s + i) * P, j, 4 * P), P), :]) for i in range(2)], d)

                gate_up(u, 0, None, outer)
                with sp.Fori(0, DOUBLE) as j:
                    d = j if outer is None else outer + j
                    gate_up(u + 2, 1, j, d)
                    down(u + 4, 0, j, d)
                    gate_up(u + 5, 2, j, d)
                    down(u + 7, 1, j, d)
                down(u + FFN_UNITS - 1, NSTEP - 1, None, outer)

            sp.dma_start(X[:], a["x"][0].rearrange("(t p) c -> p t c", p=P)).then_inc(x_in, 16)
            w_in = a["conv_w_in"][0]
            for j in range(4):
                for kh in range(2):
                    pair(U_CONV_IN + 2 * j + kh, w_in, slice(j * STEP, (j + 1) * STEP),
                         w_in, slice(D + j * STEP, D + (j + 1) * STEP), 4 * kh)
            for i in range(4):
                tall(U_CONV_OUT + i, a["conv_w_out"][0], 2 * i)
            ffn(U_FFN1, a["ffn_w_gate"][0], a["ffn_w_up"][0], a["ffn_w_down"][0])
            for i in range(4):
                tall(U_K + i, a["w_kvf"], 2 * i)
            for i in range(4):
                tall(U_V + i, a["w_kvf"], 2 * i, c0=D)
            for i in range(4):
                tall(U_Q + i, a["w_q"][0], 2 * i)
            for i in range(4):
                tall(U_WO + i, a["w_o"][0], 2 * i)
            wg = a["moe_w_gate"][0].rearrange("e k c -> (e k) c")
            wu = a["moe_w_up"][0].rearrange("e k c -> (e k) c")
            wd = a["moe_w_down"][0].rearrange("e k c -> (e k) c")
            with sp.Fori(0, E // 2) as pr:
                for b in range(2):
                    ffn(U_MOE + b * FFN_UNITS,
                        wg[bass.ds(pr * (2 * D) + b * D, D), :], wu[bass.ds(pr * (2 * D) + b * D, D), :],
                        wd[bass.ds(pr * (2 * F) + b * F, F), :], outer=pr * NSTEP)
            s = U_POOL % RING
            load(U_POOL, [(raw[:, s, g * 1024:(g + 1) * 1024].rearrange("p (g k c) -> p g k c", g=2, k=2),
                           a["pool_w_2"][0][2 * g:2 * g + 2].rearrange("g (k p) c -> p g k c", p=P)) for g in range(2)])
            ffn(U_FFN2A, a["ffn_w_in_2"][0], a["ffn_w_in_2"][0], a["ffn_w_out_2"][0], up_at=F)
            wqkv = a["attn_w_qkv_2"][0]
            for i in range(4):
                tall(U_Q2 + i, wqkv, 2 * i)
            for kh in range(2):
                pair(U_KV2 + kh, wqkv, slice(D, D + 256), wqkv, slice(D + 256, D + 512), 4 * kh)
            for i in range(4):
                tall(U_WO2 + i, a["attn_w_o_2"][0], 2 * i)
            ffn(U_FFN2B, a["ffn_w_in_2"][1], a["ffn_w_in_2"][1], a["ffn_w_out_2"][1], up_at=F)
            for t in range(T):
                sp.wait_ge(y_ready, 9 + t)
                sp.dma_start(out[0, t * P:(t + 1) * P, :], Y["low"][:, t, :]).then_inc(out_done, 16)
            sp.wait_ge(out_done, 16 * T)

        @block.gpsimd
        def _(pool):
            n = [0]

            def link(ins):
                n[0] += 1
                ins.then_inc(pool_chain, 1)
                pool.wait_ge(pool_chain, n[0])

            link(pool.memset(ident[:], 0.0))
            pool.affine_select(out=ident[:], in_=ident[:], compare_op=ALU.not_equal, fill=1.0, base=0,
                               pattern=[[-1, P]], channel_multiplier=1).then_inc(ident_ready, 1)
            link(pool.memset(ones[:], 1.0))
            link(pool.memset(tri[:], 1.0))
            link(pool.affine_select(out=tri[:], in_=tri[:], compare_op=ALU.is_ge, fill=0.0, base=0,
                                    pattern=[[1, S]], channel_multiplier=-1))
            link(pool.memset(mask[:], 0.0))
            link(pool.affine_select(out=mask[:], in_=mask[:], compare_op=ALU.is_ge, fill=NEG, base=P,
                                    pattern=[[-1, S]], channel_multiplier=1))
            link(pool.memset(ind[:], 0.0))
            link(pool.memset(dsel[:], 0.0))
            for half in range(2):
                for which in range(2):
                    base = -(64 * half + 16 * which)
                    link(pool.affine_select(out=ind[:, which, :], in_=ind[:, which, :], compare_op=ALU.not_equal,
                                            fill=1.0, base=base, pattern=[[-1, 16]], channel_multiplier=1))
                    link(pool.affine_select(out=dsel[:], in_=dsel[:], compare_op=ALU.not_equal,
                                            fill=1.0, base=base - half, pattern=[[-2, 8]], channel_multiplier=1))
            pool.iota(iota8[:], [[1, E]], base=0, channel_multiplier=0,
                      allow_small_or_imprecise_dtypes=True).then_inc(consts_ready, 1)
            pool.wait_ge(cum_ps, 1)
            pool.iota(order[:], [[1, S]], base=1, channel_multiplier=0,
                      allow_small_or_imprecise_dtypes=True).then_inc(consts_ready, 1)
            pool.wait_ge(sc_max, 8)
            link(pool.iota(dist[:], [[1, S]], base=-P, channel_multiplier=-1, allow_small_or_imprecise_dtypes=True))
            link(pool.affine_select(out=dist[:], in_=dist[:], compare_op=ALU.is_ge, fill=NEG, base=P,
                                    pattern=[[-1, S]], channel_multiplier=1))
            pool.affine_select(out=dist[:], in_=dist[:], compare_op=ALU.is_ge, fill=NEG, base=-1,
                               pattern=[[1, S]], channel_multiplier=-1).then_inc(consts_ready, 1)

        @block.scalar
        def _(act):
            n = [0]
            done = [0]

            def link(ins):
                n[0] += 1
                ins.then_inc(act_chain, 1)
                act.wait_ge(act_chain, n[0])

            def split(u, d=None):
                s = u % RING
                act.wait_ge(raw_in[s], lin(32 * (u // RING + 1), d, 32))
                if d is not None or u >= RING:
                    act.wait_ge(unit_used, lin(u - RING + 1, d, 6))
                act.activation(whi[:, s, :], raw[:, s, :], ACT.Copy).then_inc(hi_done, 1)

            def split_to(u):
                for v in range(done[0], min(u, U_END)):
                    split(v)
                done[0] = max(done[0], u)

            def norm_hi(k, gain, dst, again=0):
                for c in range(KC):
                    act.wait_ge(xt_ps, 4 * k + c // 2 + 1)
                    if again:
                        act.wait_ge(xt_lo, KC * (again - 1) + c // 2 * 2 + 2)
                    act.activation(dst[:, c, :], ps[:, c // 2, (c % 2) * S:(c % 2 + 1) * S], ACT.Copy,
                                   scale=V[:, gain + c:gain + c + 1]).then_inc(xt_hi, 1)

            def vector_load(n, free):
                act.wait_ge(bc_free, free)
                act.dma_start(bc[:, BC[n][0], :], spread(BC[n][1], D)).then_inc(bc_in, 16)

            def ahead(v, d, last):
                if last is None or v < last:
                    split(v, d)

            def step_glu(g, v, d, last):
                k = kinds["glu"]
                p = g % 2
                act.wait_ge(k["ps"], lin(g + 1, d, 2))
                act.activation(SG[:], ps[:, 2 * p, :].rearrange("p (f s) -> p f s", f=2), ACT.Silu).then_inc(k["silu"], 1)
                ahead(v + 4, d, last)
                act.wait_ge(k["mul"], lin(g + 1, d, 2))
                act.activation(hh[:, p, :, :], Ht[:], ACT.Copy).then_inc(k["hi"], 1)
                ahead(v + 5, d, last)
                ahead(v + 6, d, last)

            def step_cglu(g, v, d, last):
                k = kinds["cglu"]
                p = g % 2
                act.wait_ge(k["ps"], lin(g + 1, d, 2))
                if g in (0, NSTEP):
                    act.wait_ge(pads, 3 + g // NSTEP)
                act.activation(U2[:, 0:2, 2:2 + S], ps[:, 2 * p, :].rearrange("p (f s) -> p f s", f=2), ACT.Copy)
                act.activation(U2[:, 2:4, 2:2 + S], ps[:, 2 * p + 1, :].rearrange("p (f s) -> p f s", f=2),
                               ACT.Copy).then_inc(k["copy"], 1)
                ahead(v + 4, d, last)
                act.wait_ge(k["conv"], lin(g + 1, d, 2))
                act.activation(SG[:], C2[:, 2:4, :], ACT.Silu).then_inc(k["silu"], 1)
                ahead(v + 5, d, last)
                act.wait_ge(k["mul"], lin(g + 1, d, 2))
                act.activation(hh[:, p, :, :], Ht[:], ACT.Copy).then_inc(k["hi"], 1)
                ahead(v + 6, d, last)

            def ffn(step, u, g, outer=None, last=None):
                step(g, u, outer, last)
                with act.Fori(0, DOUBLE - (last is not None)) as j:
                    d = j if outer is None else outer + j
                    step(g + 1, u + 3, d, last)
                    step(g + 2, u + 6, d, last)
                if last is not None:
                    q = DOUBLE - 1
                    step(g + 1 + 2 * q, u + 3 + 6 * q, None, last)
                    step(g + 2 + 2 * q, u + 6 + 6 * q, None, last)

            def straight_ffn(step, u, g, last=None):
                split_to(u + 4)
                ffn(step, u, g, None, last)
                done[0] = min(u + FFN_UNITS + 4, U_END)

            for at, v, m in vector_rows():
                act.dma_start(stage[at % P:at % P + m, at // P, :], v).then_inc(vec_in, 16)
            act.dma_start(wf_raw[:], a["w_kvf"][:, 2 * D:2 * D + H].rearrange("(k p) c -> p k c", p=P)).then_inc(small_in, 16)
            act.dma_start(wr_raw[:], a["router_w"][0].rearrange("(k p) c -> p k c", p=P)).then_inc(small_in, 16)
            act.dma_start(bf[:], spread(a["b_f"], H)).then_inc(small_in, 16)
            act.dma_start(rb[:], spread(a["router_b"], E)).then_inc(small_in, 16)
            act.dma_start(sink[:], spread(a["attn_sinks_2"], H)).then_inc(small_in, 16)
            act.dma_start(bc[:, 0, :], spread(BC[0][1], D)).then_inc(bc_in, 16)
            act.dma_start(bc[:, 1, :], spread(BC[1][1], D)).then_inc(bc_in, 16)

            act.wait_ge(vec_ps, 1)
            act.activation(V[:], ps[:, 6:8, :].rearrange("p b c -> p (b c)")[:, 0:NCOL], ACT.Copy).then_inc(vec_ready, 1)
            split_to(2)
            act.wait_ge(vec_ready, 1)
            norm_hi(0, COL["mix_norm"], xh)
            split_to(6)

            for j in range(4):
                act.wait_ge(cin_ps, j + 1)
                if j >= 1:
                    act.wait_ge(cin_mul, j)
                for f in range(2):
                    col = COL["conv_b_in"] + KC + 2 * j + f
                    ins = act.activation(SGc[:, f, :], ps[:, 2 * (j % 2) + 1, f * S:(f + 1) * S], ACT.Sigmoid,
                                         bias=V[:, col:col + 1])
                ins.then_inc(cin_sig, 1)
                split_to(2 * j + 8)
            act.wait_ge(centered, 1)
            act.activation(Z[:], C[:], ACT.Square).then_inc(squared, 1)
            act.wait_ge(scaled, 1)
            for c in range(KC):
                ins = act.activation(Z[:, c, :], C[:, c, :], ACT.Silu, bias=V[:, COL["conv_ln_b"] + c:COL["conv_ln_b"] + c + 1],
                                     scale=V[:, COL["conv_ln_g"] + c:COL["conv_ln_g"] + c + 1])
            link(ins)
            act.activation(xh[:], Z[:], ACT.Copy).then_inc(z_ready, 1)
            act.wait_ge(small_in, 16 * 5)
            act.activation(wf[:, 0, :, :], wf_raw[:], ACT.Copy).then_inc(small_hi, 1)
            act.activation(wr[:, 0, :, :], wr_raw[:], ACT.Copy).then_inc(small_hi, 1)

            norm_hi(1, COL["ffn_norm"], xh)
            straight_ffn(step_glu, U_FFN1, 0)
            vector_load(2, 1)

            norm_hi(2, COL["kv_norm"], hnh)
            norm_hi(2, COL["mix_norm"] + KC, xh, again=3)
            split_to(U_K + 6)

            def take_qk(i, dst, bias=None):
                act.wait_ge(qk_ps, i + 1)
                for c in range(KC):
                    src = ps[:, c // 2, (c % 2) * S:(c % 2 + 1) * S]
                    if bias is None:
                        ins = act.activation(dst[:, c, :], src, ACT.Copy)
                    else:
                        ins = act.activation(dst[:, c, :], src, ACT.Identity, bias=V[:, bias + c:bias + c + 1])
                ins.then_inc(qk_out, 1)

            take_qk(0, kT)
            split_to(U_V + 6)
            act.wait_ge(f_z, 1)
            link(act.activation(fz[:, 1, :, :], fz[:, 1, :, :], ACT.Exp, scale=-1.0))
            act.activation(fz[:, 2, :, :], fz[:, 1, :, :], ACT.Ln, bias=1.0).then_inc(f_ln, 1)
            act.wait_ge(acc_ps, 3)
            split_to(U_Q + 6)
            take_qk(1, qT)

            def attention(n0, layer):
                for g in range(8):
                    K = P if g < 4 else S
                    G = n0 + g
                    act.wait_ge(sc_max, G + 1)
                    for h in range(4):
                        ins = act.activation(SC[:, h, 0:K], SC[:, h, 0:K], ACT.Exp, bias=nmax[:, g, h:h + 1],
                                             scale=HD ** -0.5, accum_out=rsum[:, g, h:h + 1])
                        if layer == 1:
                            hd = 4 * (g % 4) + h
                            ins = act.activation(esink[:, g, h:h + 1], sink[:, hd:hd + 1], ACT.Exp, bias=nmax[:, g, h:h + 1])
                    ins.then_inc(sc_exp, 1)
                    if g >= 4:
                        act.wait_ge(pt_ps, G + 1)
                        act.activation(PT[:, 1, :, :], ps[:, 5, :].rearrange("p (h q) -> p h q", h=4), ACT.Copy).then_inc(pt_a, 1)
                    act.wait_ge(o_ps, G + 1)
                    c0, q0 = 2 * (g % 4), (g // 4) * P
                    act.activation(xh[:, c0:c0 + 2, q0:q0 + P], ps[:, 6, 0:2 * P].rearrange("p (c q) -> p c q", c=2),
                                   ACT.Copy).then_inc(o_hi, 1)

            split_to(U_WO + 6)
            attention(0, 0)

            norm_hi(3, COL["ffn_norm"] + KC, xh)
            split_to(U_MOE + 4)
            act.wait_ge(r_top, 1)
            act.activation(gl[:, 2, :, 0:1], gl[:, 2, :, 0:1], ACT.Exp).then_inc(r_exp, 1)
            with act.Fori(0, E // 2) as pr:
                for b in range(2):
                    ffn(step_glu, U_MOE + b * FFN_UNITS, NSTEP * (1 + b), outer=pr * NSTEP)
            done[0] = U_POOL + 4

            act.wait_ge(pads, 2)
            for c in range(KC):
                act.wait_ge(xt_ps, 4 * 4 + c // 2 + 1)
                ins = act.activation(HF[:, c, MAXW:MAXW + S], ps[:, c // 2, (c % 2) * S:(c % 2 + 1) * S], ACT.Copy,
                                     scale=V[:, COL["norm_mix_2"] + c:COL["norm_mix_2"] + c + 1])
            ins.then_inc(hf_ready, 1)
            vector_load(3, 2)
            act.wait_ge(po_ready, 1)
            act.activation(xh[:], PO[:], ACT.Copy).then_inc(z_ready, 1)
            norm_hi(5, COL["norm_ffn_2"], xh)
            straight_ffn(step_cglu, U_FFN2A, 0)
            vector_load(4, 3)
            act.dma_start(bv2, a["attn_b_qkv_2"][0:1, D + 256:D + 512].to_broadcast([P, 256])).then_inc(bc_in, 16)

            norm_hi(6, COL["norm_mix_2"] + KC, xh)
            split_to(U_Q2 + 6)
            take_qk(2, qT, bias=COL["attn_b_qkv_2"])
            split_to(U_Q2 + 10)
            act.wait_ge(qk_ps, 4)
            for kv in range(KVH):
                col = COL["attn_b_qkv_2"] + KC + kv // 2
                r = 64 * (kv % 2)
                for half in range(2):
                    ins = act.activation(kT2[64 * half:64 * half + 64, kv, :], ps[r:r + 64, 4, (kv // 2) * S:(kv // 2 + 1) * S],
                                         ACT.Identity, bias=V[r:r + 64, col:col + 1])
            ins.then_inc(qk_out, 1)
            split_to(U_WO2 + 6)
            attention(8, 1)
            norm_hi(7, COL["norm_ffn_2"] + KC, xh)
            straight_ffn(step_cglu, U_FFN2B, NSTEP, last=U_END)

        @block.vector
        def _(dve):
            n = [0]
            done = [0]
            norms = [0]
            lows = [0]

            def link(ins):
                n[0] += 1
                ins.then_inc(dve_chain, 1)
                dve.wait_ge(dve_chain, n[0])

            def split(u, d=None):
                s = u % RING
                dve.wait_ge(hi_done, lin(u + 1, d, 6))
                dve.tensor_tensor(wlo[:, s, :], raw[:, s, :], whi[:, s, :].bitcast(F32), ALU.subtract).then_inc(lo_done, 1)

            def split_to(u):
                for v in range(done[0], min(u, U_END)):
                    split(v)
                done[0] = max(done[0], u)

            def rsqrt(r, v, t):
                link(dve.tensor_scalar(t.bitcast(U32), v.bitcast(U32), 1, None, ALU.logical_shift_right))
                link(dve.tensor_scalar(r.bitcast(I32), t.bitcast(I32), -1.0, float(0x5F3759DF), ALU.mult, ALU.add))
                for _ in range(3):
                    link(dve.tensor_tensor(t, r, r, ALU.mult))
                    link(dve.scalar_tensor_tensor(t, t, -0.5, v, ALU.mult, ALU.mult))
                    link(dve.scalar_tensor_tensor(r, t, 1.5, r, ALU.add, ALU.mult))

            def rms(where):
                for t in range(T):
                    ins = dve.tensor_tensor_reduce(junk[where][:], X[:, t, :], X[:, t, :], 1.0, 0.0, ALU.mult, ALU.add,
                                                   st[:, t:t + 1])
                    link(ins)
                link(dve.tensor_scalar(st[:, 2:4], st[:, 0:2], 1.0 / D, EPS, ALU.mult, ALU.add))
                rsqrt(st[:, 4:6], st[:, 2:4], st[:, 6:8])

            def norm(where):
                rms(where)
                for t in range(T):
                    ins = dve.tensor_scalar(Y[where][:, t, :], X[:, t, :], st[:, 4 + t:5 + t], None, ALU.mult)
                ins.then_inc(y_ready, 1)
                norms[0] += 1

            def norm_lo(gain, src_hi, dst):
                for c in range(KC):
                    dve.wait_ge(xt_hi, KC * lows[0] + c // 2 * 2 + 2)
                    dve.scalar_tensor_tensor(dst[:, c, :], ps[:, c // 2, (c % 2) * S:(c % 2 + 1) * S],
                                             V[:, gain + c:gain + c + 1], src_hi[:, c, :].bitcast(F32),
                                             ALU.mult, ALU.subtract).then_inc(xt_lo, 1)
                lows[0] += 1

            def acc(t):
                return ps[:, 4 + 2 * t:6 + 2 * t, :].rearrange("p b c -> p (b c)")

            def add_acc(k):
                dve.wait_ge(acc_ps, k + 1)
                for t in range(T):
                    ins = dve.tensor_tensor(X[:, t, :], acc(t), X[:, t, :], ALU.add)
                ins.then_inc(acc_free, 1)
                dve.wait_ge(acc_free, k + 1)

            def ahead(v, d, last):
                if last is None or v < last:
                    split(v, d)

            def step_glu(g, s, v, d, j, last):
                k = kinds["glu"]
                p = g % 2
                dve.wait_ge(k["silu"], lin(g + 1, d, 2))
                if g:
                    dve.wait_ge(k["lo"], lin(g, d, 2))
                dve.tensor_tensor(Ht[:], SG[:], ps[:, 2 * p + 1, :].rearrange("p (f s) -> p f s", f=2),
                                  ALU.mult).then_inc(k["mul"], 1)
                ahead(v + 4, d, last)
                dve.wait_ge(k["hi"], lin(g + 1, d, 2))
                dve.tensor_tensor(hl[:, p, :, :], Ht[:], hh[:, p, :, :].bitcast(F32), ALU.subtract).then_inc(k["lo"], 1)
                ahead(v + 5, d, last)
                ahead(v + 6, d, last)

            def step_cglu(g, s, v, d, j, last):
                k = kinds["cglu"]
                p = g % 2
                layer = g // NSTEP
                dve.wait_ge(k["copy"], lin(g + 1, d, 2))
                if g:
                    dve.wait_ge(k["mul"], lin(g, d, 2))
                for tap in (2, 1, 0):
                    for f in range(4):
                        chunk = 2 * s + f % 2 + (F // P) * (f // 2)
                        at = COL["ffn_conv_w_2"] + (layer * CTAPS + tap) * 44 + chunk
                        w = V[:, at:at + 1] if j is None else V[:, bass.ds(j * 4 + at, 1)]
                        op = (2 - tap) * 4 + f
                        if tap == 2:
                            at = COL["ffn_conv_b_2"] + layer * 44 + chunk
                            b = V[:, at:at + 1] if j is None else V[:, bass.ds(j * 4 + at, 1)]
                            ins = dve.tensor_scalar(C2[:, f, :], U2[:, f, 2:2 + S], w, b, ALU.mult, ALU.add)
                        else:
                            dve.wait_ge(k["tap"], lin(12 * g + op - 3, d, 24))
                            ins = dve.scalar_tensor_tensor(C2[:, f, :], U2[:, f, tap:tap + S], w, C2[:, f, :],
                                                           ALU.mult, ALU.add)
                        ins.then_inc(k["tap"], 1)
                dve.wait_ge(k["tap"], lin(12 * g + 12, d, 24))
                dve.sem_inc(k["conv"], 1)
                ahead(v + 4, d, last)
                dve.wait_ge(k["silu"], lin(g + 1, d, 2))
                if g:
                    dve.wait_ge(k["lo"], lin(g, d, 2))
                dve.tensor_tensor(Ht[:], SG[:], C2[:, 0:2, :], ALU.mult).then_inc(k["mul"], 1)
                ahead(v + 5, d, last)
                dve.wait_ge(k["hi"], lin(g + 1, d, 2))
                dve.tensor_tensor(hl[:, p, :, :], Ht[:], hh[:, p, :, :].bitcast(F32), ALU.subtract).then_inc(k["lo"], 1)
                ahead(v + 6, d, last)

            def ffn(step, u, g, outer=None, last=None):
                step(g, 0, u, outer, None, last)
                with dve.Fori(0, DOUBLE - (last is not None)) as j:
                    d = j if outer is None else outer + j
                    step(g + 1, 1, u + 3, d, j, last)
                    step(g + 2, 2, u + 6, d, j, last)
                if last is not None:
                    q = DOUBLE - 1
                    step(g + 1 + 2 * q, 1 + 2 * q, u + 3 + 6 * q, None, None, last)
                    step(g + 2 + 2 * q, 2 + 2 * q, u + 6 + 6 * q, None, None, last)

            def straight_ffn(step, u, g, last=None):
                split_to(u + 4)
                ffn(step, u, g, None, last)
                done[0] = min(u + FFN_UNITS + 4, U_END)

            dve.wait_ge(x_in, 16)
            norm("low")
            split_to(2)
            dve.wait_ge(vec_ready, 1)
            norm_lo(COL["mix_norm"], xh, xl)
            dve.memset(U[:, :, 0:PAD], 0.0).then_inc(pads, 1)
            split_to(6)
            dve.wait_ge(bc_in, 32)
            for t in range(T):
                ins = dve.tensor_tensor(X[:, t, :], X[:, t, :], bc[:, 0, :], ALU.add)
            ins.then_inc(bc_free, 1)
            dve.wait_ge(consts_ready, 1)
            dve.tensor_reduce(rows[:], ind[:], AX_X, ALU.add)
            dve.wait_ge(pads, 1)

            for j in range(4):
                dve.wait_ge(cin_sig, j + 1)
                for f in range(2):
                    c = 2 * j + f
                    col = COL["conv_b_in"] + c
                    ins = dve.scalar_tensor_tensor(U[:, c, PAD:PAD + S], ps[:, 2 * (j % 2), f * S:(f + 1) * S], V[:, col:col + 1],
                                                   SGc[:, f, :], ALU.add, ALU.mult)
                ins.then_inc(cin_mul, 1)
                split_to(2 * j + 8)
                dve.wait_ge(cin_mul, j + 1)
                base = 2 * TAPS * j
                for f in range(2):
                    c = 2 * j + f
                    w, b = COL["conv_w_dw"] + c, COL["conv_b_dw"] + c
                    dve.tensor_scalar(C[:, c, :], U[:, c, 0:S], V[:, w:w + 1], V[:, b:b + 1], ALU.mult, ALU.add).then_inc(tap_done, 1)
                with dve.Fori(0, PAD // 5) as i:
                    for q in range(5):
                        for f in range(2):
                            c = 2 * j + f
                            dve.wait_ge(tap_done, i * 10 + (base + 2 * q + f + 1))
                            dve.scalar_tensor_tensor(C[:, c, :], U[:, c, bass.ds(i * 5 + (q + 1), S)],
                                                     V[:, bass.ds(i * (5 * KC) + (COL["conv_w_dw"] + (q + 1) * KC + c), 1)],
                                                     C[:, c, :], ALU.mult, ALU.add).then_inc(tap_done, 1)
                dve.wait_ge(tap_done, base + 2 * TAPS)
                dve.sem_inc(conv_done, 1)

            def over(v, k=KC):
                return v.unsqueeze(1).to_broadcast([P, k, S])

            dve.wait_ge(stat_ps, 1)
            link(dve.tensor_scalar(MU[:], ps[:, 4, 0:S], 1.0 / D, None, ALU.mult))
            dve.tensor_tensor(C[:], C[:], over(MU), ALU.subtract).then_inc(centered, 1)
            dve.wait_ge(stat_ps, 2)
            link(dve.tensor_scalar(VAR, ps[:, 5, 0:S], 1.0 / D, EPS, ALU.mult, ALU.add))
            rsqrt(RS, VAR, MU)
            dve.wait_ge(centered, 1)
            dve.tensor_tensor(C[:], C[:], over(RS), ALU.mult).then_inc(scaled, 1)
            dve.wait_ge(z_ready, 1)
            dve.tensor_tensor(xl[:], Z[:], xh[:].bitcast(F32), ALU.subtract).then_inc(z_lo, 1)
            dve.wait_ge(small_hi, 2)
            dve.tensor_tensor(wf[:, 1, :, :], wf_raw[:], wf[:, 0, :, :].bitcast(F32), ALU.subtract)
            dve.tensor_tensor(wr[:, 1, :, :], wr_raw[:], wr[:, 0, :, :].bitcast(F32), ALU.subtract)
            dve.tensor_scalar(sink8[:], sink[:], HD ** 0.5, None, ALU.mult).then_inc(small_lo, 1)
            add_acc(0)

            norm("low")
            norm_lo(COL["ffn_norm"], xh, xl)
            straight_ffn(step_glu, U_FFN1, 0)
            add_acc(1)

            norm("high")
            norm_lo(COL["kv_norm"], hnh, hnl)
            norm_lo(COL["mix_norm"] + KC, xh, xl)
            split_to(U_K + 6)
            dve.wait_ge(f_ps, 1)
            link(dve.tensor_tensor(fz[:, 0, :, :], ps[:, 4, 0:T * H].rearrange("p (t h) -> p t h", t=T),
                                   bf[:].unsqueeze(1).to_broadcast([P, T, H]), ALU.add))
            dve.scalar_tensor_tensor(fz[:, 1, :, :], fz[:, 0, :, :], -1.0, fz[:, 0, :, :], ALU.mult, ALU.max).then_inc(f_z, 1)
            dve.tensor_scalar(fz[:, 3, :, :], fz[:, 0, :, :], 0.0, None, ALU.min)
            split_to(U_V + 6)
            link(dve.memset(Lc[:], 0.0))
            dve.wait_ge(f_ln, 1)
            link(dve.tensor_tensor(fz[:, 3, :, :], fz[:, 3, :, :], fz[:, 2, :, :], ALU.subtract))
            for half in range(2):
                for which, s in ((0, HD ** 0.5), (1, -(HD ** 0.5))):
                    at = 64 * half + 16 * which
                    ins = dve.tensor_scalar(Lc[:, :, at:at + H], fz[:, 3, :, :], s, None, ALU.mult)
            ins.then_inc(cum_in, 1)
            dve.wait_ge(acc_ps, 3)
            for t in range(T):
                ins = dve.tensor_copy(vt[:, t, :], acc(t))
            ins.then_inc(acc_free, 1)
            split_to(U_Q + 6)
            dve.wait_ge(cum_ps, 1)
            dve.tensor_scalar(Mq[:], ps[:, 4, 0:S], rows[:, 0:1], rows[:, 1:2], ALU.mult, ALU.add)
            dve.tensor_scalar(Mk[:], ps[:, 4, 0:S], rows[:, 1:2], rows[:, 0:1], ALU.mult, ALU.add).then_inc(cum_ready, 1)
            dve.wait_ge(cum_ready, 1)
            split_to(U_WO + 6)

            def attention(n0, layer):
                def spread_term(g):
                    if g >= 2:
                        dve.wait_ge(sc_ps, n0 + g - 1)
                    q0 = (g // 4) * P
                    for pr in range(2):
                        pair_ = 2 * (g % 4) + pr
                        ins = dve.tensor_scalar(MH[:, g % 2, pr, :], Mq[:, q0:q0 + P], dsel[:, pair_:pair_ + 1], None, ALU.mult)
                    ins.then_inc(mh_ready, 1)

                if layer == 0:
                    spread_term(0)
                for g in range(8):
                    G = n0 + g
                    K = P if g < 4 else S
                    if layer == 0 and g < 7:
                        spread_term(g + 1)
                    dve.wait_ge(sc_ps, G + 1)
                    if G % 8:
                        dve.wait_ge(pt_ps, G)
                    for odd in range(2):
                        src = ps[:, 2 * (g % 2) + odd, 0:2 * K].rearrange("p (h k) -> p h k", h=2)
                        if layer == 0:
                            ins = dve.tensor_tensor(SC[:, odd::2, 0:K], src, mask[:, S - K:S].unsqueeze(1).to_broadcast([P, 2, K]),
                                                    ALU.add)
                        else:
                            for i in range(2):
                                slope = 2.0 ** (-8.0 / H * (4 * (g % 4) + 2 * i + odd + 1))
                                ins = dve.scalar_tensor_tensor(SC[:, 2 * i + odd, 0:K], dist[:, S - K:S], slope * HD ** 0.5,
                                                               src[:, i, :], ALU.mult, ALU.add)
                    link(ins)
                    link(dve.tensor_reduce(rmax[:, g, :], SC[:, :, 0:K], AX_X, ALU.max))
                    if layer == 1:
                        link(dve.tensor_tensor(rmax[:, g, :], rmax[:, g, :], sink8[:, 4 * (g % 4):4 * (g % 4) + 4], ALU.max))
                    dve.tensor_scalar(nmax[:, g, :], rmax[:, g, :], -(HD ** -0.5), None, ALU.mult).then_inc(sc_max, 1)
                    dve.wait_ge(sc_exp, G + 1)
                    if layer == 1:
                        link(dve.tensor_tensor(rsum[:, g, :], rsum[:, g, :], esink[:, g, :], ALU.add))
                    link(dve.reciprocal(rinv[:, g, :], rsum[:, g, :]))
                    dve.tensor_tensor(SC[:, :, 0:K], SC[:, :, 0:K], rinv[:, g, :].unsqueeze(2).to_broadcast([P, 4, K]),
                                      ALU.mult).then_inc(sc_norm, 1)
                    dve.wait_ge(pt_ps, G + 1)
                    if G % 8:
                        dve.wait_ge(o_ps, G)
                    dve.tensor_copy(PT[:, 0, :, :], ps[:, 4, :].rearrange("p (h q) -> p h q", h=4)).then_inc(pt_v, 1)
                    dve.wait_ge(o_hi, G + 1)
                    c0, q0 = 2 * (g % 4), (g // 4) * P
                    dve.tensor_tensor(xl[:, c0:c0 + 2, q0:q0 + P], ps[:, 6, 0:2 * P].rearrange("p (c q) -> p c q", c=2),
                                      xh[:, c0:c0 + 2, q0:q0 + P].bitcast(F32), ALU.subtract).then_inc(o_lo, 1)

            attention(0, 0)
            add_acc(3)

            norm("low")
            norm_lo(COL["ffn_norm"] + KC, xh, xl)
            split_to(U_MOE + 4)
            dve.wait_ge(r_ps, 1)
            link(dve.tensor_tensor(gl[:, 0, :, :], ps[:, 4, 0:T * E].rearrange("p (t e) -> p t e", t=T),
                                   rb[:].unsqueeze(1).to_broadcast([P, T, E]), ALU.add))
            for t in range(T):
                link(dve.max(gl[:, 1, t, :], gl[:, 0, t, :]))
                link(dve.max_index(gi[:, t, :], gl[:, 1, t, :], gl[:, 0, t, :]))
            dve.tensor_copy(gl[:, 3, :, :], gi[:])
            dve.tensor_tensor(gl[:, 2, :, 0:1], gl[:, 1, :, 1:2], gl[:, 1, :, 0:1], ALU.subtract).then_inc(r_top, 1)
            dve.wait_ge(r_exp, 1)
            link(dve.tensor_scalar(gl[:, 2, :, 1:2], gl[:, 2, :, 0:1], 1.0, None, ALU.add))
            link(dve.reciprocal(gl[:, 2, :, 2:3], gl[:, 2, :, 1:2]))
            link(dve.tensor_tensor(gl[:, 2, :, 3:4], gl[:, 2, :, 0:1], gl[:, 2, :, 2:3], ALU.mult))
            for t in range(T):
                dve.tensor_scalar(gate[:, t, :], iota8[:], gl[:, 3, t, 0:1], gl[:, 2, t, 2:3], ALU.is_equal, ALU.mult)
                link(dve.tensor_scalar(gl[:, 0, t, :], iota8[:], gl[:, 3, t, 1:2], gl[:, 2, t, 3:4], ALU.is_equal, ALU.mult))
            link(dve.tensor_tensor(gate[:], gate[:], gl[:, 0, :, :], ALU.add))

            with dve.Fori(0, E // 2) as pr:
                for b in range(2):
                    ffn(step_glu, U_MOE + b * FFN_UNITS, NSTEP * (1 + b), outer=pr * NSTEP)
                    dve.wait_ge(acc_ps, pr * 2 + (4 + b + 1))
                    for t in range(T):
                        ins = dve.scalar_tensor_tensor(X[:, t, :], acc(t), gate[:, t, bass.ds(pr * 2 + b, 1)], X[:, t, :],
                                                       ALU.mult, ALU.add)
                    ins.then_inc(acc_free, 1)
                    dve.wait_ge(acc_free, pr * 2 + (4 + b + 1))
            done[0] = U_POOL + 4

            rms("low")
            for t in range(T):
                ins = dve.scalar_tensor_tensor(X[:, t, :], X[:, t, :], st[:, 4 + t:5 + t], bc[:, 1, :], ALU.mult, ALU.mult)
            ins.then_inc(bc_free, 1)
            dve.wait_ge(bc_free, 2)

            norm("low")
            dve.wait_ge(consts_ready, 2)
            for w in range(4):
                ins = dve.tensor_scalar(count[:, w, :], order[:], float(WINDOWS[w]), None, ALU.min)
            link(ins)
            link(dve.reciprocal(count[:], count[:]))
            dve.memset(SA[:], 0.0)
            dve.memset(SB[:], 0.0)
            dve.memset(HF[:, :, 0:MAXW], 0.0).then_inc(pads, 1)
            dve.wait_ge(pads, 2)
            dve.wait_ge(hf_ready, 1)
            for g, win in enumerate(WINDOWS):
                c = 2 * g
                src = HF[:, c:c + 2, :]
                nxt = [SA, SB]
                width = 1
                while width < win:
                    dst = nxt[0]
                    link(dve.tensor_tensor(dst[:, :, MAXW:], src[:, :, MAXW:], src[:, :, MAXW - width:MAXW + S - width], ALU.add))
                    src, nxt, width = dst, nxt[::-1], 2 * width
                link(dve.tensor_tensor(src[:, :, MAXW:], src[:, :, MAXW:], over(count[:, g, :], 2), ALU.mult))
                ins = dve.tensor_tensor(PO[:, c:c + 2, :], src[:, :, MAXW:], HF[:, c:c + 2, MAXW:], ALU.subtract)
                link(ins) if g < 3 else ins.then_inc(po_ready, 1)
            dve.wait_ge(z_ready, 2)
            dve.tensor_tensor(xl[:], PO[:], xh[:].bitcast(F32), ALU.subtract).then_inc(z_lo, 1)
            dve.wait_ge(acc_ps, 13)
            dve.wait_ge(bc_in, 64)
            for t in range(T):
                link(dve.tensor_tensor(Y["low"][:, t, :], acc(t), bc[:, 0, :], ALU.add))
                link(dve.tensor_tensor(Y["low"][:, t, :], Y["low"][:, t, :], bc[:, 1, :], ALU.mult))
                ins = dve.tensor_tensor(X[:, t, :], X[:, t, :], Y["low"][:, t, :], ALU.add)
                if t == 0:
                    link(ins)
            ins.then_inc(bc_free, 1)
            dve.wait_ge(bc_free, 3)
            dve.sem_inc(acc_free, 1)

            def conv_ffn(u, layer, k, last=None):
                norm("low")
                norm_lo(COL["norm_ffn_2"] + layer * KC, xh, xl)
                dve.memset(U2[:, :, 0:2], 0.0).then_inc(pads, 1)
                straight_ffn(step_cglu, u, layer * NSTEP, last)
                add_acc(k)

            conv_ffn(U_FFN2A, 0, 13)

            norm("low")
            norm_lo(COL["norm_mix_2"] + KC, xh, xl)
            split_to(U_Q2 + 10)
            dve.wait_ge(qk_ps, 4)
            dve.wait_ge(bc_in, 16 * 6)
            for t in range(T):
                ins = dve.tensor_tensor(vt2[:, t, :], ps[:, 6 + t, 0:256], bv2, ALU.add)
            ins.then_inc(v2_ready, 1)
            split_to(U_WO2 + 6)
            dve.wait_ge(consts_ready, 3)
            attention(8, 1)
            add_acc(14)
            conv_ffn(U_FFN2B, 1, 15, last=U_END)
            rms("low")
            for t in range(T):
                dve.scalar_tensor_tensor(Y["low"][:, t, :], X[:, t, :], st[:, 4 + t:5 + t], bc[:, 0, :], ALU.mult,
                                         ALU.mult).then_inc(y_ready, 1)

        @block.tensor
        def _(pe):
            def norm_t(k, where):
                pe.wait_ge(y_ready, k + 1)
                for c in range(KC):
                    for t in range(T):
                        at = (c % 2) * S + t * P
                        ins = pe.transpose(ps[:, c // 2, at:at + P], Y[where][:, t, c * P:(c + 1) * P], ident[:])
                    if c % 2:
                        ins.then_inc(xt_ps, 1)

            def feat(dst, s, cols, h, l, start, stop=False):
                pe.matmul(dst, whi[:, s, cols], h, start=start, stop=False, skip_group_check=True)
                pe.matmul(dst, whi[:, s, cols], l, start=False, stop=False, skip_group_check=True)
                return pe.matmul(dst, wlo[:, s, cols], h, start=False, stop=stop, skip_group_check=True)

            def toks(dst, s, cols, h, l, start, stop):
                pe.matmul(dst, h, whi[:, s, cols], start=start, stop=False, skip_group_check=True)
                pe.matmul(dst, l, whi[:, s, cols], start=False, stop=False, skip_group_check=True)
                return pe.matmul(dst, h, wlo[:, s, cols], start=False, stop=stop, skip_group_check=True)

            def split_in(u, d=None):
                pe.wait_ge(lo_done, lin(u + 1, d, 6))

            def gate_up(u, p, d):
                for kh in range(2):
                    split_in(u + kh, d)
                    s = (u + kh) % RING
                    for f in range(4):
                        for k in range(4):
                            kk = 4 * kh + k
                            c0 = k * 2 * STEP + f * P
                            ins = feat(ps[:, 2 * p + f // 2, (f % 2) * S:(f % 2 + 1) * S], s, slice(c0, c0 + P),
                                       xh[:, kk, :], xl[:, kk, :], start=(kk == 0 and f % 2 == 0), stop=(kk == KC - 1))
                    ins.then_inc(unit_used, 1)
                return ins

            def token_major(k, u, n=4, after=None, h=xh, l=xl):
                pe.wait_ge(acc_free, k)
                for i in range(n):
                    split_in(u + i)
                    s = (u + i) % RING
                    for kk in range(2):
                        c = 2 * i + kk
                        for t in range(T):
                            for half in range(2):
                                c0 = kk * D + half * 512
                                ins = toks(ps[:, 4 + 2 * t + half, :], s, slice(c0, c0 + 512), h[:, c, t * P:(t + 1) * P],
                                           l[:, c, t * P:(t + 1) * P], start=(c == 0), stop=(c == 2 * n - 1))
                    ins.then_inc(unit_used, 1)
                pe.wait_ge(unit_used, u + n)
                pe.sem_inc(acc_ps, 1)

            def feat_major(i, u, h=xh, l=xl):
                for q in range(4):
                    split_in(u + q)
                    s = (u + q) % RING
                    for kk in range(2):
                        k = 2 * q + kk
                        for c in range(KC):
                            c0 = kk * D + c * P
                            ins = feat(ps[:, c // 2, (c % 2) * S:(c % 2 + 1) * S], s, slice(c0, c0 + P), h[:, k, :], l[:, k, :],
                                       start=(k == 0 and c % 2 == 0), stop=(k == KC - 1))
                    ins.then_inc(unit_used, 1)
                pe.wait_ge(unit_used, u + 4)
                pe.sem_inc(qk_ps, 1)

            def down(k, g, u, d, first=False):
                pe.wait_ge(k["lo"], lin(g + 1, d, 2))
                split_in(u, d)
                s = u % RING
                p = g % 2
                for f in range(2):
                    for t in range(T):
                        for half in range(2):
                            c0 = f * D + half * 512
                            ins = toks(ps[:, 4 + 2 * t + half, :], s, slice(c0, c0 + 512), hh[:, p, f, t * P:(t + 1) * P],
                                       hl[:, p, f, t * P:(t + 1) * P], start=(first and f == 0), stop=False)
                ins.then_inc(unit_used, 1)

            def ffn(kind, u, g, k, outer=None, kd=None):
                sems = kinds[kind]
                read = sems["mul"] if kind == "glu" else sems["copy"]

                def up(g, u, d):
                    if d is not None or g >= 2:
                        pe.wait_ge(read, lin(g - 1, d, 2))
                    gate_up(u, g % 2, d)
                    pe.wait_ge(unit_used, lin(u + 2, d, 6))
                    pe.sem_inc(sems["ps"], 1)

                def double(g, u, d, first=False):
                    up(g, u, d)
                    if first:
                        pe.wait_ge(acc_free, k if kd is None else kd * 2 + k)
                    down(sems, g - 1, u + 2, d, first)
                    up(g + 1, u + 3, d)
                    down(sems, g, u + 5, d)

                up(g, u, outer)
                double(g + 1, u + 2, outer, first=True)
                with pe.Fori(1, DOUBLE) as j:
                    double(g + 1, u + 2, j if outer is None else outer + j)
                down(sems, g + NSTEP - 1, u + FFN_UNITS - 1, outer)
                pe.wait_ge(unit_used, lin(u + FFN_UNITS, outer, 6))
                pe.sem_inc(acc_ps, 1)

            def normed(evac):
                pe.wait_ge(xt_lo, KC * (evac + 1))

            pe.wait_ge(ident_ready, 1)
            pe.wait_ge(vec_in, 16 * len(vector_rows()))
            for b in range(NBLK):
                m = min(P, NCOL - b * P)
                ins = pe.transpose(ps[:, 6 + b // 4, (b % 4) * P:(b % 4) * P + m], stage[0:m, b, :], ident[0:m, 0:m])
            ins.then_inc(vec_ps, 1)

            norm_t(0, "low")
            normed(0)
            for j in range(4):
                if j >= 2:
                    pe.wait_ge(cin_mul, j - 1)
                gate_up(U_CONV_IN + 2 * j, j % 2, None)
                pe.wait_ge(unit_used, 2 * j + 2)
                pe.sem_inc(cin_ps, 1)
            pe.wait_ge(consts_ready, 1)
            for c in range(KC):
                pe.wait_ge(conv_done, c // 2 + 1)
                ins = pe.matmul(ps[:, 4, 0:S], ones[:], C[:, c, :], start=(c == 0), stop=(c == KC - 1))
            ins.then_inc(stat_ps, 1)
            pe.wait_ge(squared, 1)
            for c in range(KC):
                ins = pe.matmul(ps[:, 5, 0:S], ones[:], Z[:, c, :], start=(c == 0), stop=(c == KC - 1))
            ins.then_inc(stat_ps, 1)
            pe.wait_ge(z_lo, 1)
            token_major(0, U_CONV_OUT)

            norm_t(1, "low")
            normed(1)
            ffn("glu", U_FFN1, 0, 1)

            norm_t(2, "high")
            normed(3)
            feat_major(0, U_K, hnh, hnl)
            pe.wait_ge(small_lo, 1)
            for t in range(T):
                dst = ps[:, 4, t * H:(t + 1) * H]
                for c in range(KC):
                    h_, l_ = hnh[:, c, t * P:(t + 1) * P], hnl[:, c, t * P:(t + 1) * P]
                    pe.matmul(dst, h_, wf[:, 0, c, :], start=(c == 0), stop=False)
                    pe.matmul(dst, l_, wf[:, 0, c, :], start=False, stop=False)
                    ins = pe.matmul(dst, h_, wf[:, 1, c, :], start=False, stop=(c == KC - 1))
            ins.then_inc(f_ps, 1)
            pe.wait_ge(f_z, 1)
            token_major(2, U_V, h=hnh, l=hnl)
            pe.wait_ge(qk_out, 1)
            feat_major(1, U_Q)
            pe.wait_ge(acc_free, 3)
            pe.wait_ge(cum_in, 1)
            pe.matmul(ps[:, 4, 0:S], Lc[:, 0, :], tri[:], start=True, stop=False)
            pe.matmul(ps[:, 4, P:S], Lc[:, 1, :], tri[:, 0:P], start=False, stop=True).then_inc(cum_ps, 1)

            def attention(n0, layer):
                def scores(g):
                    G = n0 + g
                    K = P if g < 4 else S
                    q0 = (g // 4) * P
                    if g >= 2:
                        pe.wait_ge(sc_max, G - 1)
                    if layer == 0:
                        pe.wait_ge(mh_ready, g + 1)
                    for h in range(4):
                        hd = 4 * (g % 4) + h
                        r = 64 * (h % 2)
                        dst = ps[:, 2 * (g % 2) + h % 2, (h // 2) * K:(h // 2 + 1) * K]
                        keys = kT[r:r + 64, hd // 2, 0:K] if layer == 0 else kT2[r:r + 64, g % 4, 0:K]
                        ins = pe.matmul(dst, qT[r:r + 64, hd // 2, q0:q0 + P], keys, start=True, stop=(layer == 1))
                        if layer == 0:
                            ins = pe.matmul(dst, MH[r:r + 64, g % 2, h // 2, :], Mk[r:r + 64, 0:K], start=False, stop=True)
                    ins.then_inc(sc_ps, 1)

                scores(0)
                for g in range(8):
                    G = n0 + g
                    nk = 1 if g < 4 else 2
                    if g < 7:
                        scores(g + 1)
                    pe.wait_ge(sc_norm, G + 1)
                    for kc in range(nk):
                        for h in range(4):
                            ins = pe.transpose(ps[:, 4 + kc, h * P:(h + 1) * P], SC[:, h, kc * P:(kc + 1) * P], ident[:])
                    ins.then_inc(pt_ps, 1)
                    pe.wait_ge(pt_v, G + 1)
                    if g >= 4:
                        pe.wait_ge(pt_a, 4 * layer + g - 3)
                    if g:
                        pe.wait_ge(o_lo, G)
                    for h in range(4):
                        hd = 4 * (g % 4) + h
                        for kc in range(nk):
                            vals = vt[:, kc, hd * HD:(hd + 1) * HD] if layer == 0 else vt2[:, kc, (g % 4) * HD:(g % 4 + 1) * HD]
                            ins = pe.matmul(ps[64 * (h % 2):64 * (h % 2) + 64, 6, (h // 2) * P:(h // 2 + 1) * P], vals,
                                            PT[:, kc, h, :], start=(kc == 0), stop=(kc == nk - 1))
                    ins.then_inc(o_ps, 1)
                pe.wait_ge(o_lo, n0 + 8)

            pe.wait_ge(qk_out, 2)
            pe.wait_ge(cum_ready, 1)
            attention(0, 0)
            token_major(3, U_WO)

            norm_t(3, "low")
            normed(4)
            for t in range(T):
                dst = ps[:, 4, t * E:(t + 1) * E]
                for c in range(KC):
                    h_, l_ = xh[:, c, t * P:(t + 1) * P], xl[:, c, t * P:(t + 1) * P]
                    pe.matmul(dst, h_, wr[:, 0, c, :], start=(c == 0), stop=False)
                    pe.matmul(dst, l_, wr[:, 0, c, :], start=False, stop=False)
                    ins = pe.matmul(dst, h_, wr[:, 1, c, :], start=False, stop=(c == KC - 1))
            ins.then_inc(r_ps, 1)
            with pe.Fori(0, E // 2) as pr:
                for b in range(2):
                    ffn("glu", U_MOE + b * FFN_UNITS, NSTEP * (1 + b), 4 + b, outer=pr * NSTEP, kd=pr)

            norm_t(4, "low")
            pe.wait_ge(z_lo, 2)
            pe.wait_ge(acc_free, 12)
            split_in(U_POOL)
            for t in range(T):
                for g in range(4):
                    for k in range(2):
                        c0 = g * 512 + k * 256
                        ins = toks(ps[:, 4 + 2 * t + g // 2, (g % 2) * 256:(g % 2 + 1) * 256], U_POOL % RING, slice(c0, c0 + 256),
                                   xh[:, 2 * g + k, t * P:(t + 1) * P], xl[:, 2 * g + k, t * P:(t + 1) * P],
                                   start=(k == 0), stop=(k == 1))
            ins.then_inc(unit_used, 1)
            pe.wait_ge(unit_used, U_POOL + 1)
            pe.sem_inc(acc_ps, 1)
            norm_t(5, "low")
            normed(5)
            ffn("cglu", U_FFN2A, 0, 13)

            norm_t(6, "low")
            normed(6)
            feat_major(2, U_Q2)
            for kh in range(2):
                split_in(U_KV2 + kh)
                s = (U_KV2 + kh) % RING
                for k in range(4):
                    kk = 4 * kh + k
                    for f in range(2):
                        c0 = k * 512 + f * P
                        feat(ps[:, 4, f * S:(f + 1) * S], s, slice(c0, c0 + P), xh[:, kk, :], xl[:, kk, :],
                             start=(kk == 0 and f == 0), stop=(kk == KC - 1))
                    for t in range(T):
                        ins = toks(ps[:, 6 + t, 0:256], s, slice(k * 512 + 256, k * 512 + 512), xh[:, kk, t * P:(t + 1) * P],
                                   xl[:, kk, t * P:(t + 1) * P], start=(kk == 0), stop=(kk == KC - 1))
                ins.then_inc(unit_used, 1)
            pe.wait_ge(unit_used, U_KV2 + 2)
            pe.sem_inc(qk_ps, 1)
            pe.wait_ge(qk_out, 4)
            pe.wait_ge(v2_ready, 1)
            attention(8, 1)
            token_major(14, U_WO2)
            norm_t(7, "low")
            normed(7)
            ffn("cglu", U_FFN2B, NSTEP, 15)


_INS = ['x', 'mix_norm', 'ffn_norm', 'conv_w_in', 'conv_b_in', 'conv_w_dw', 'conv_b_dw', 'conv_ln_g', 'conv_ln_b',
        'conv_w_out', 'conv_b_out', 'kv_norm', 'w_kvf', 'b_f', 'w_q', 'w_o', 'ffn_w_gate', 'ffn_w_up', 'ffn_w_down',
        'router_w', 'router_b', 'moe_w_gate', 'moe_w_up', 'moe_w_down', 'final_norm', 'pool_w_2', 'pool_b_2',
        'pool_scale_2', 'attn_w_qkv_2', 'attn_b_qkv_2', 'attn_sinks_2', 'attn_w_o_2', 'norm_mix_2', 'norm_ffn_2',
        'ffn_w_in_2', 'ffn_conv_w_2', 'ffn_conv_b_2', 'ffn_w_out_2', 'norm_f_2']


def kernel(**inputs):
    import numpy as _np
    import concourse.bacc as _bacc
    from concourse import mybir as _mybir
    from concourse.bass_utils import run_bass_kernel_spmd as _run

    nc = _bacc.Bacc("TRN2", target_bir_lowering=False, num_devices=1, dynamic_dma_scratch_size=1024)
    arrays, args = {}, {}
    for name in _INS:
        v = _np.ascontiguousarray(inputs[name])
        arrays[f"in_{name}_dram"] = v
        args[name] = nc.dram_tensor(f"in_{name}_dram", v.shape, _mybir.dt.from_np(v.dtype), kind="ExternalInput").ap()
    out = nc.dram_tensor("out_0_dram", (1, S, D), F32, kind="ExternalOutput").ap()
    build(nc, args, out)
    r = _run(nc, [arrays], core_ids=[0])
    return r.results[0]["out_0_dram"]
```

```python
import math
from contextlib import ExitStack

import concourse.bass as bass
from concourse import mybir

F32 = mybir.dt.float32
F32R = mybir.dt.float32r
U32 = mybir.dt.uint32
I32 = mybir.dt.int32
ALU = mybir.AluOpType
ACT = mybir.ActivationFunctionType
AX_X = mybir.AxisListType.X

P = 128
D = 1024
S = 256
T = S // P
KC = D // P
F = 2816
STEP = 256
NSTEP = F // STEP
DOUBLE = (NSTEP - 1) // 2
E = 8
H = 16
HD = 64
KVH = 4
TAPS = 31
PAD = TAPS - 1
PE_TAPS = 13
V_TAPS = TAPS - PE_TAPS
DIAGS = 8
PE_TURNS = (PE_TAPS - 1) * 2 // DIAGS
V_TURNS = (V_TAPS - 2) // 4
assert PE_TURNS * DIAGS == 2 * (PE_TAPS - 1) and 4 * V_TURNS == V_TAPS - 2
SLOTS = P
OVER = 2 * S // (SLOTS + 1)
CTAPS = 3
WINDOWS = (2, 4, 8, 16)
MAXW = max(WINDOWS)
EPS = 1e-6
NEG = -1e30
RING = 6
WORK = 9216
UNIT = 2048
FFN_UNITS = 3 * NSTEP

U_CONV_IN = 0
U_CONV_OUT = U_CONV_IN + 8
U_FFN1 = U_CONV_OUT + 4
U_K = U_FFN1 + FFN_UNITS
U_V = U_K + 4
U_Q = U_V + 4
U_WO = U_Q + 4
U_MOE = U_WO + 4
U_POOL = U_MOE + E * FFN_UNITS
U_FFN2A = U_POOL + 1
U_Q2 = U_FFN2A + FFN_UNITS
U_KV2 = U_Q2 + 4
U_WO2 = U_KV2 + 2
U_FFN2B = U_WO2 + 4
U_END = U_FFN2B + FFN_UNITS

VECTORS = [("mix_norm", 16), ("ffn_norm", 16), ("kv_norm", 8), ("conv_b_in", 16), ("conv_w_dw", 8 * TAPS),
           ("conv_b_dw", 8), ("conv_ln_g", 8), ("conv_ln_b", 8), ("norm_mix_2", 16), ("norm_ffn_2", 16),
           ("attn_b_qkv_2", 12), ("ffn_conv_w_2", 2 * CTAPS * 44), ("ffn_conv_b_2", 2 * 44)]
COL, _n = {}, 0
for _name, _rows in VECTORS:
    COL[_name] = _n
    _n += _rows
NCOL = _n
NBLK = -(-NCOL // P)


def lin(base, d, per):
    return base if d is None else d * per + base


def build(nc, a, out):
    with ExitStack() as ctx:
        def sb(name, shape, dt=F32):
            return ctx.enter_context(nc.sbuf_tensor(name, shape, dt))

        def sem(name):
            return ctx.enter_context(nc.semaphore(name))

        ps = ctx.enter_context(nc.psum_tensor("ps", [P, 8, 512], F32))
        work_at = -(-nc.sbuf_base // 32) * 32
        work = sb("work", [P, WORK])
        assert nc.sbuf_base == work_at + 4 * WORK
        raw = sb("raw", [P, RING, UNIT])
        whi = sb("whi", [P, RING, UNIT], F32R)
        wlo = sb("wlo", [P, RING, UNIT], F32R)
        X = sb("X", [P, T, D])
        xh = sb("xh", [P, KC, S], F32R)
        xl = sb("xl", [P, KC, S], F32R)
        V = sb("V", [P, NCOL])
        bc = sb("bc", [P, 2, D])
        ident = sb("ident", [P, P])
        ones = sb("ones", [P, P])
        tri = sb("tri", [P, S])
        order = tri
        mask = sb("mask", [P, S])
        dist = mask
        ind = sb("ind", [P, 2, 16])
        rows = sb("rows", [P, 2])
        dsel = sb("dsel", [P, 8])
        iota8 = sb("iota8", [P, E])
        wf_raw = sb("wf_raw", [P, KC, H])
        wf = sb("wf", [P, 2, KC, H], F32R)
        wr_raw = sb("wr_raw", [P, KC, E])
        wr = sb("wr", [P, 2, KC, E], F32R)
        bf = sb("bf", [P, H])
        rb = sb("rb", [P, E])
        sink = sb("sink", [P, H])
        sink8 = sb("sink8", [P, H])
        bv2 = bc[:, 1, 0:256]
        st = sb("st", [P, 64])
        fz = sb("fz", [P, 4, T, H])
        gate = sb("gate", [P, T, E + 2])
        rank = sb("rank", [P, T, E + 2])
        gate_o = sb("gate_o", [P, T, OVER])
        rank_o = sb("rank_o", [P, T, OVER])
        over = sb("over", [P, 1 + OVER], I32)
        gl = sb("gl", [P, 4, T, E])
        gi = sb("gi", [P, T, 8], U32)
        rmax = sb("rmax", [P, 8, 4])
        nmax = sb("nmax", [P, 8, 4])
        rsum = sb("rsum", [P, 8, 4])
        esink = sb("esink", [P, 8, 4])
        rinv = sb("rinv", [P, 8, 4])

        def wk(at, *shape):
            n = math.prod(shape)
            v = work[:, at:at + n]
            if len(shape) == 2:
                return v.rearrange("p (a b) -> p a b", b=shape[1])
            if len(shape) == 3:
                return v.rearrange("p (a b c) -> p a b c", b=shape[1], c=shape[2])
            return v

        def wkr(name, at, *shape):
            return nc.alloc_sbuf_tensor_at(name, [P, *shape], F32R, offset=work_at + 4 * at)

        Y = {"low": wk(0, T, D), "high": wk(4096, T, D)}
        junk = {"low": wk(2048, D), "high": wk(6144, D)}
        U = wk(0, KC, PAD + S)
        SGc = wk(2304, 2, S)
        C = wk(3072, KC, S)
        MU = wk(5120, S)
        RS = wk(5376, S)
        VAR = wk(7680, S)
        Z = wk(5632, KC, S)
        diag = wk(5632, DIAGS + 2, P)
        stage = wk(8192, NBLK, P)
        SG = wk(0, 2, S)
        Ht = wk(512, 2, S)
        hh = wkr("hh", 1024, 2, 2, S)
        hl = wkr("hl", 2048, 2, 2, S)
        U2 = wk(3072, 4, 2 + S)
        C2 = wk(4104, 4, S)
        Yh = wkr("Yh", 2048, T, D)
        Yl = wkr("Yl", 4096, T, D)
        SGm = wk(0, STEP)
        Hm = wk(256, STEP)
        th = wkr("th", 512, 2, 2, SLOTS)
        tl = wkr("tl", 1024, 2, 2, SLOTS)
        Pm = wkr("Pm", 1536, T, SLOTS)
        yh = wkr("yh", 6144, D)
        yl = wkr("yl", 7168, D)
        PTr = wkr("PTr", 8192, 2, S)
        identr = wkr("identr", 8704, P)
        rt = wk(8832, 48, 8)
        wA = bc[:, 0, :]
        wB = wk(7168, D)
        xo = wk(6144, KC, SLOTS)
        yo = wk(6144, D)
        SGo = wk(0, P)
        Ho = wk(256, P)
        to = wk(1792, SLOTS)
        PTo = wk(8192, S)
        hnh = wkr("hnh", 0, KC, S)
        hnl = wkr("hnl", 2048, KC, S)
        qT = wk(0, KC, S)
        SC = wk(2048, 4, S)
        PT = wk(3072, 2, 4, P)
        kT = wk(4096, KC, S)
        vt = wk(6144, T, D)
        Mq = wk(8192, S)
        Mk = wk(8448, S)
        MH = wk(8704, 2, 2, P)
        Lc = wk(8704, T, P)
        kT2 = wk(4096, KVH, S)
        vt2 = wk(6144, T, 256)
        edge = wk(8448, 4, MAXW)
        HF = wk(3072, KC, MAXW + S)
        SA = wk(5248, 2, MAXW + S)
        SB = wk(5792, 2, MAXW + S)
        PO = wk(6400, KC, S)

        x_in = sem("x_in")
        vec_in = sem("vec_in")
        small_in = sem("small_in")
        bc_in = sem("bc_in")
        bc_free = sem("bc_free")
        out_done = sem("out_done")
        ident_ready = sem("ident_ready")
        consts_ready = sem("consts_ready")
        pool_chain = sem("pool_chain")
        dve_chain = sem("dve_chain")
        act_chain = sem("act_chain")
        vec_ps = sem("vec_ps")
        vec_ready = sem("vec_ready")
        raw_in = [sem(f"raw_in{s}") for s in range(RING)]
        hi_done = sem("hi_done")
        lo_done = sem("lo_done")
        unit_used = sem("unit_used")
        x_final = sem("x_final")
        squares = sem("squares")
        y_ready = sem("y_ready")
        xt_ps = sem("xt_ps")
        xt_hi = sem("xt_hi")
        xt_lo = sem("xt_lo")
        acc_ps = sem("acc_ps")
        acc_free = sem("acc_free")
        cin_ps = sem("cin_ps")
        cin_sig = sem("cin_sig")
        cin_mul = sem("cin_mul")
        tap_done = sem("tap_done")
        diag_free = sem("diag_free")
        diag_ready = sem("diag_ready")
        conv_ps = sem("conv_ps")
        conv_done = sem("conv_done")
        stat_ps = sem("stat_ps")
        centered = sem("centered")
        squared = sem("squared")
        scaled = sem("scaled")
        z_ready = sem("z_ready")
        kinds = {}
        for kind in ("glu", "cglu"):
            kinds[kind] = {n: sem(f"{kind}_{n}") for n in ("ps", "copy", "conv", "tap", "silu", "mul", "hi", "lo")}
        kinds["moe"] = {n: sem(f"moe_{n}") for n in ("ps", "silu", "mul", "t", "hi", "lo")}
        rows_hi = sem("rows_hi")
        rows_lo = sem("rows_lo")
        sel_ready = sem("sel_ready")
        rank_ps = sem("rank_ps")
        perm_ready = sem("perm_ready")
        permt_ps = sem("permt_ps")
        permt_ready = sem("permt_ready")
        gather_ps = sem("gather_ps")
        gather_hi = sem("gather_hi")
        gather_lo = sem("gather_lo")
        y_ps = sem("y_ps")
        y_hi = sem("y_hi")
        y_lo = sem("y_lo")
        comb_ps = sem("comb_ps")
        comb_add = sem("comb_add")
        over_ready = sem("over_ready")
        ov = {n: sem(f"ov_{n}") for n in ("perm", "permt", "pt", "gather", "x", "gu_in", "gu", "silu", "mul", "t", "h",
                                           "down_in", "down", "y", "comb", "add")}
        small_hi = sem("small_hi")
        small_lo = sem("small_lo")
        qk_ps = sem("qk_ps")
        qk_out = sem("qk_out")
        f_ps = sem("f_ps")
        f_z = sem("f_z")
        f_ln = sem("f_ln")
        cum_in = sem("cum_in")
        cum_ps = sem("cum_ps")
        cum_ready = sem("cum_ready")
        mh_ready = sem("mh_ready")
        sc_ps = sem("sc_ps")
        sc_max = sem("sc_max")
        sc_exp = sem("sc_exp")
        sc_norm = sem("sc_norm")
        pt_ps = sem("pt_ps")
        pt_a = sem("pt_a")
        pt_v = sem("pt_v")
        o_ps = sem("o_ps")
        o_hi = sem("o_hi")
        o_lo = sem("o_lo")
        r_ps = sem("r_ps")
        r_top = sem("r_top")
        r_exp = sem("r_exp")
        pads = sem("pads")
        z_lo = sem("z_lo")
        v2_ready = sem("v2_ready")
        hf_ready = sem("hf_ready")
        po_ready = sem("po_ready")

        block = ctx.enter_context(nc.Block())

        BC = [(0, a["conv_b_out"]), (1, a["final_norm"]), (0, a["ffn_norm"][1]), (0, a["pool_b_2"]), (1, a["pool_scale_2"]),
              (0, a["norm_f_2"])]

        FC = F // P
        moe_gate = a["moe_w_gate"][0].rearrange("e k c -> (e k) c")
        moe_up = a["moe_w_up"][0].rearrange("e k c -> (e k) c")
        moe_down = a["moe_w_down"][0].rearrange("e k c -> (e k) c")

        def spread(v, n):
            flat = v
            while len(flat.shape) > 1:
                names = "abcd"[:len(flat.shape)]
                flat = flat.rearrange(f"{' '.join(names)} -> ({' '.join(names)})")
            return flat[0:n].unsqueeze(0).to_broadcast([P, n])

        def vector_rows():
            pieces = []
            for name, nrow in VECTORS:
                v = a[name]
                names = "abcd"[:len(v.shape)]
                v = v.rearrange(f"{' '.join(names)} -> ({' '.join(names)})").rearrange("(r c) -> r c", c=P)
                r = 0
                while r < nrow:
                    at = COL[name] + r
                    m = min(nrow - r, P - at % P)
                    pieces.append((at, v[r:r + m, :], m))
                    r += m
            return pieces

        @block.sync
        def _(sp):
            def kmaj(w, k0, nk, c0, nc_):
                return w[k0 * P:(k0 + nk) * P, c0:c0 + nc_].rearrange("(k p) c -> p k c", p=P)

            def load(u, parts, d=None):
                s = u % RING
                if d is not None or u >= RING:
                    sp.wait_ge(lo_done, lin(u - RING + 1, d, 6))
                for dst, src in parts:
                    sp.dma_start(dst, src).then_inc(raw_in[s], 16)

            def tall(u, w, k0, c0=0, d=None):
                s = u % RING
                load(u, [(raw[:, s, i * D:(i + 1) * D], w[(k0 + i) * P:(k0 + i + 1) * P, c0:c0 + D]) for i in range(2)], d)

            def pair(u, wa, ca, wb, cb, k0, d=None):
                v = raw[:, u % RING, :].rearrange("p (k h c) -> p k h c", k=4, h=2)
                load(u, [(v[:, :, h, :], w[k0 * P:(k0 + 4) * P, c].rearrange("(k p) c -> p k c", p=P))
                         for h, w, c in ((0, wa, ca), (1, wb, cb))], d)

            def ffn(u, wg, wu, wd, shift=0, up_at=0, outer=None):
                def gate_up(u, s, j, d):
                    col = lin(s * STEP, j, 2 * STEP)
                    colu = lin(s * STEP + up_at, j, 2 * STEP)
                    for kh in range(2):
                        pair(u + kh, wg, bass.ds(col, STEP), wu, bass.ds(colu, STEP), 4 * kh, d)

                def down(u, s, j, d):
                    r = u % RING
                    load(u, [(raw[:, r, i * D:(i + 1) * D], wd[bass.ds(lin((2 * s + i) * P, j, 4 * P), P), :]) for i in range(2)], d)

                gate_up(u, 0, None, outer)
                with sp.Fori(0, DOUBLE) as j:
                    d = j if outer is None else outer + j
                    gate_up(u + 2, 1, j, d)
                    down(u + 4, 0, j, d)
                    gate_up(u + 5, 2, j, d)
                    down(u + 7, 1, j, d)
                down(u + FFN_UNITS - 1, NSTEP - 1, None, outer)

            sp.dma_start(X[:], a["x"][0].rearrange("(t p) c -> p t c", p=P)).then_inc(x_in, 16)
            w_in = a["conv_w_in"][0]
            for j in range(4):
                for kh in range(2):
                    pair(U_CONV_IN + 2 * j + kh, w_in, slice(j * STEP, (j + 1) * STEP),
                         w_in, slice(D + j * STEP, D + (j + 1) * STEP), 4 * kh)
            for i in range(4):
                tall(U_CONV_OUT + i, a["conv_w_out"][0], 2 * i)
            ffn(U_FFN1, a["ffn_w_gate"][0], a["ffn_w_up"][0], a["ffn_w_down"][0])
            for i in range(4):
                tall(U_K + i, a["w_kvf"], 2 * i)
            for i in range(4):
                tall(U_V + i, a["w_kvf"], 2 * i, c0=D)
            for i in range(4):
                tall(U_Q + i, a["w_q"][0], 2 * i)
            for i in range(4):
                tall(U_WO + i, a["w_o"][0], 2 * i)
            with sp.Fori(0, E // 2) as pr:
                for b in range(2):
                    ffn(U_MOE + b * FFN_UNITS,
                        moe_gate[bass.ds(pr * (2 * D) + b * D, D), :], moe_up[bass.ds(pr * (2 * D) + b * D, D), :],
                        moe_down[bass.ds(pr * (2 * F) + b * F, F), :], outer=pr * NSTEP)
            s = U_POOL % RING
            load(U_POOL, [(raw[:, s, g * 1024:(g + 1) * 1024].rearrange("p (g k c) -> p g k c", g=2, k=2),
                           a["pool_w_2"][0][2 * g:2 * g + 2].rearrange("g (k p) c -> p g k c", p=P)) for g in range(2)])
            ffn(U_FFN2A, a["ffn_w_in_2"][0], a["ffn_w_in_2"][0], a["ffn_w_out_2"][0], up_at=F)
            wqkv = a["attn_w_qkv_2"][0]
            for i in range(4):
                tall(U_Q2 + i, wqkv, 2 * i)
            for kh in range(2):
                pair(U_KV2 + kh, wqkv, slice(D, D + 256), wqkv, slice(D + 256, D + 512), 4 * kh)
            for i in range(4):
                tall(U_WO2 + i, a["attn_w_o_2"][0], 2 * i)
            ffn(U_FFN2B, a["ffn_w_in_2"][1], a["ffn_w_in_2"][1], a["ffn_w_out_2"][1], up_at=F)
            for t in range(T):
                sp.wait_ge(y_ready, 9 + t)
                sp.dma_start(out[0, t * P:(t + 1) * P, :], Y["low"][:, t, :]).then_inc(out_done, 16)
            sp.wait_ge(out_done, 16 * T)

        @block.gpsimd
        def _(pool):
            n = [0]

            def link(ins):
                n[0] += 1
                ins.then_inc(pool_chain, 1)
                pool.wait_ge(pool_chain, n[0])

            link(pool.memset(ident[:], 0.0))
            pool.affine_select(out=ident[:], in_=ident[:], compare_op=ALU.not_equal, fill=1.0, base=0,
                               pattern=[[-1, P]], channel_multiplier=1).then_inc(ident_ready, 1)
            link(pool.memset(ones[:], 1.0))
            link(pool.memset(tri[:], 1.0))
            link(pool.affine_select(out=tri[:], in_=tri[:], compare_op=ALU.is_ge, fill=0.0, base=0,
                                    pattern=[[1, S]], channel_multiplier=-1))
            link(pool.memset(mask[:], 0.0))
            link(pool.affine_select(out=mask[:], in_=mask[:], compare_op=ALU.is_ge, fill=NEG, base=P,
                                    pattern=[[-1, S]], channel_multiplier=1))
            link(pool.memset(ind[:], 0.0))
            link(pool.memset(dsel[:], 0.0))
            for half in range(2):
                for which in range(2):
                    base = -(64 * half + 16 * which)
                    link(pool.affine_select(out=ind[:, which, :], in_=ind[:, which, :], compare_op=ALU.not_equal,
                                            fill=1.0, base=base, pattern=[[-1, 16]], channel_multiplier=1))
                    link(pool.affine_select(out=dsel[:], in_=dsel[:], compare_op=ALU.not_equal,
                                            fill=1.0, base=base - half, pattern=[[-2, 8]], channel_multiplier=1))
            pool.iota(iota8[:], [[1, E]], base=0, channel_multiplier=0,
                      allow_small_or_imprecise_dtypes=True).then_inc(consts_ready, 1)
            pool.wait_ge(rank_ps, 1)
            pool.iota(order[:], [[1, S]], base=1, channel_multiplier=0,
                      allow_small_or_imprecise_dtypes=True).then_inc(consts_ready, 1)
            pool.wait_ge(sc_max, 8)
            link(pool.iota(dist[:], [[1, S]], base=-P, channel_multiplier=-1, allow_small_or_imprecise_dtypes=True))
            link(pool.affine_select(out=dist[:], in_=dist[:], compare_op=ALU.is_ge, fill=NEG, base=P,
                                    pattern=[[-1, S]], channel_multiplier=1))
            pool.affine_select(out=dist[:], in_=dist[:], compare_op=ALU.is_ge, fill=NEG, base=-1,
                               pattern=[[1, S]], channel_multiplier=-1).then_inc(consts_ready, 1)

        @block.scalar
        def _(act):
            n = [0]
            done = [0]

            def link(ins):
                n[0] += 1
                ins.then_inc(act_chain, 1)
                act.wait_ge(act_chain, n[0])

            def split(u, d=None):
                s = u % RING
                act.wait_ge(raw_in[s], lin(32 * (u // RING + 1), d, 32))
                if d is not None or u >= RING:
                    act.wait_ge(unit_used, lin(u - RING + 1, d, 6))
                act.activation(whi[:, s, :], raw[:, s, :], ACT.Copy).then_inc(hi_done, 1)

            def split_to(u):
                for v in range(done[0], min(u, U_END)):
                    split(v)
                done[0] = max(done[0], u)

            def norm_hi(k, gain, dst, again=0):
                for c in range(KC):
                    act.wait_ge(xt_ps, 4 * k + c // 2 + 1)
                    if again:
                        act.wait_ge(xt_lo, KC * (again - 1) + c // 2 * 2 + 2)
                    act.activation(dst[:, c, :], ps[:, c // 2, (c % 2) * S:(c % 2 + 1) * S], ACT.Copy,
                                   scale=V[:, gain + c:gain + c + 1]).then_inc(xt_hi, 1)

            sums = [0]

            def square(where):
                sums[0] += 1
                act.wait_ge(x_final, sums[0])
                act.activation(Y[where][:, 0, :], X[:, 0, :], ACT.Square, accum_out=st[:, 0:1]).then_inc(squares, 1)

            def vector_load(n, free):
                act.wait_ge(bc_free, free)
                act.dma_start(bc[:, BC[n][0], :], spread(BC[n][1], D)).then_inc(bc_in, 16)

            def ahead(v, d, last):
                if last is None or v < last:
                    split(v, d)

            def step_glu(g, v, d, last):
                k = kinds["glu"]
                p = g % 2
                act.wait_ge(k["ps"], lin(g + 1, d, 2))
                act.activation(SG[:], ps[:, 2 * p, :].rearrange("p (f s) -> p f s", f=2), ACT.Silu).then_inc(k["silu"], 1)
                ahead(v + 4, d, last)
                act.wait_ge(k["mul"], lin(g + 1, d, 2))
                act.activation(hh[:, p, :, :], Ht[:], ACT.Copy).then_inc(k["hi"], 1)
                ahead(v + 5, d, last)
                ahead(v + 6, d, last)

            def step_cglu(g, v, d, last):
                k = kinds["cglu"]
                p = g % 2
                act.wait_ge(k["ps"], lin(g + 1, d, 2))
                if g in (0, NSTEP):
                    act.wait_ge(pads, 3 + g // NSTEP)
                act.activation(U2[:, 0:2, 2:2 + S], ps[:, 2 * p, :].rearrange("p (f s) -> p f s", f=2), ACT.Copy)
                act.activation(U2[:, 2:4, 2:2 + S], ps[:, 2 * p + 1, :].rearrange("p (f s) -> p f s", f=2),
                               ACT.Copy).then_inc(k["copy"], 1)
                ahead(v + 4, d, last)
                act.wait_ge(k["conv"], lin(g + 1, d, 2))
                act.activation(SG[:], C2[:, 2:4, :], ACT.Silu).then_inc(k["silu"], 1)
                ahead(v + 5, d, last)
                act.wait_ge(k["mul"], lin(g + 1, d, 2))
                act.activation(hh[:, p, :, :], Ht[:], ACT.Copy).then_inc(k["hi"], 1)
                ahead(v + 6, d, last)

            def ffn(step, u, g, outer=None, last=None):
                step(g, u, outer, last)
                with act.Fori(0, DOUBLE - (last is not None)) as j:
                    d = j if outer is None else outer + j
                    step(g + 1, u + 3, d, last)
                    step(g + 2, u + 6, d, last)
                if last is not None:
                    q = DOUBLE - 1
                    step(g + 1 + 2 * q, u + 3 + 6 * q, None, last)
                    step(g + 2 + 2 * q, u + 6 + 6 * q, None, last)

            def straight_ffn(step, u, g, last=None):
                split_to(u + 4)
                ffn(step, u, g, None, last)
                done[0] = min(u + FFN_UNITS + 4, U_END)

            for at, v, m in vector_rows():
                act.dma_start(stage[at % P:at % P + m, at // P, :], v).then_inc(vec_in, 16)
            act.dma_start(wf_raw[:], a["w_kvf"][:, 2 * D:2 * D + H].rearrange("(k p) c -> p k c", p=P)).then_inc(small_in, 16)
            act.dma_start(wr_raw[:], a["router_w"][0].rearrange("(k p) c -> p k c", p=P)).then_inc(small_in, 16)
            act.dma_start(bf[:], spread(a["b_f"], H)).then_inc(small_in, 16)
            act.dma_start(rb[:], spread(a["router_b"], E)).then_inc(small_in, 16)
            act.dma_start(sink[:], spread(a["attn_sinks_2"], H)).then_inc(small_in, 16)
            act.dma_start(bc[:, 0, :], spread(BC[0][1], D)).then_inc(bc_in, 16)
            act.dma_start(bc[:, 1, :], spread(BC[1][1], D)).then_inc(bc_in, 16)

            act.wait_ge(vec_ps, 1)
            act.activation(V[:], ps[:, 6:8, :].rearrange("p b c -> p (b c)")[:, 0:NCOL], ACT.Copy).then_inc(vec_ready, 1)
            split_to(2)
            act.wait_ge(vec_ready, 1)
            norm_hi(0, COL["mix_norm"], xh)
            split_to(6)

            def diagonals(j):
                def one(slot, n, at):
                    act.wait_ge(diag_free, n + 1)
                    act.activation(diag[:, slot, :], ident[:], ACT.Copy, scale=V[:, at]).then_inc(diag_ready, 1)

                base = 2 * PE_TAPS * j
                first = COL["conv_w_dw"] + V_TAPS * KC + 2 * j
                for f in range(2):
                    one(DIAGS + f, base + f, slice(first + f, first + f + 1))
                with act.Fori(0, PE_TURNS) as i:
                    for m in range(DIAGS):
                        one(m, i * DIAGS + (base + 4 + m), bass.ds(i * (DIAGS // 2 * KC) + (first + (1 + m // 2) * KC + m % 2), 1))

            act.sem_inc(diag_free, DIAGS + 2)
            for j in range(4):
                act.wait_ge(cin_ps, j + 1)
                if j >= 1:
                    act.wait_ge(cin_mul, j)
                for f in range(2):
                    col = COL["conv_b_in"] + KC + 2 * j + f
                    ins = act.activation(SGc[:, f, :], ps[:, 2 * (j % 2) + 1, f * S:(f + 1) * S], ACT.Sigmoid,
                                         bias=V[:, col:col + 1])
                ins.then_inc(cin_sig, 1)
                if j >= 1:
                    diagonals(j - 1)
                split_to(2 * j + 8)
            diagonals(3)
            act.wait_ge(centered, 1)
            act.activation(Z[:], C[:], ACT.Square).then_inc(squared, 1)
            act.wait_ge(scaled, 1)
            for c in range(KC):
                ins = act.activation(Z[:, c, :], C[:, c, :], ACT.Silu, bias=V[:, COL["conv_ln_b"] + c:COL["conv_ln_b"] + c + 1],
                                     scale=V[:, COL["conv_ln_g"] + c:COL["conv_ln_g"] + c + 1])
            link(ins)
            act.activation(xh[:], Z[:], ACT.Copy).then_inc(z_ready, 1)
            act.wait_ge(small_in, 16 * 5)
            act.activation(wf[:, 0, :, :], wf_raw[:], ACT.Copy).then_inc(small_hi, 1)
            act.activation(wr[:, 0, :, :], wr_raw[:], ACT.Copy).then_inc(small_hi, 1)

            square("low")
            norm_hi(1, COL["ffn_norm"], xh)
            straight_ffn(step_glu, U_FFN1, 0)
            vector_load(2, 1)

            square("high")
            norm_hi(2, COL["kv_norm"], hnh)
            norm_hi(2, COL["mix_norm"] + KC, xh, again=3)
            split_to(U_K + 6)

            def take_qk(i, dst, bias=None):
                act.wait_ge(qk_ps, i + 1)
                for c in range(KC):
                    src = ps[:, c // 2, (c % 2) * S:(c % 2 + 1) * S]
                    if bias is None:
                        ins = act.activation(dst[:, c, :], src, ACT.Copy)
                    else:
                        ins = act.activation(dst[:, c, :], src, ACT.Identity, bias=V[:, bias + c:bias + c + 1])
                ins.then_inc(qk_out, 1)

            take_qk(0, kT)
            split_to(U_V + 6)
            act.wait_ge(f_z, 1)
            link(act.activation(fz[:, 1, :, :], fz[:, 1, :, :], ACT.Exp, scale=-1.0))
            act.activation(fz[:, 2, :, :], fz[:, 1, :, :], ACT.Ln, bias=1.0).then_inc(f_ln, 1)
            act.wait_ge(acc_ps, 3)
            split_to(U_Q + 6)
            take_qk(1, qT)

            def attention(n0, layer):
                def exps(g):
                    G, K = n0 + g, P if g < 4 else S
                    act.wait_ge(sc_max, G + 1)
                    if g:
                        act.wait_ge(pt_ps, G)
                    for h in range(4):
                        ins = act.activation(SC[:, h, 0:K], ps[:, 2 * (g % 2) + h % 2, (h // 2) * K:(h // 2 + 1) * K], ACT.Exp,
                                             bias=nmax[:, g, h:h + 1], scale=HD ** -0.5, accum_out=rsum[:, g, h:h + 1])
                    if layer == 1:
                        ins = act.activation(esink[:, g, :], esink[:, g, :], ACT.Exp, scale=HD ** -0.5)
                    ins.then_inc(sc_exp, 1)

                def upper(g):
                    act.wait_ge(o_ps, n0 + g + 1)
                    c0, q0 = 2 * (g % 4), (g // 4) * P
                    act.activation(xh[:, c0:c0 + 2, q0:q0 + P], ps[:, 6 + g % 2, 0:2 * P].rearrange("p (c q) -> p c q", c=2),
                                   ACT.Copy).then_inc(o_hi, 1)

                exps(0)
                for g in range(8):
                    if g:
                        upper(g - 1)
                    if g >= 4:
                        act.wait_ge(pt_ps, n0 + g + 1)
                        if g > 4:
                            act.wait_ge(o_ps, n0 + g)
                        act.activation(PT[:, 1, :, :], ps[:, 5, :].rearrange("p (h q) -> p h q", h=4), ACT.Copy).then_inc(pt_a, 1)
                    if g < 7:
                        exps(g + 1)
                upper(7)

            split_to(U_WO + 6)
            attention(0, 0)

            square("low")
            for b in range(4):
                act.wait_ge(xt_ps, 4 * 3 + b + 1)
                act.activation(xh[:, 2 * b:2 * b + 2, :], ps[:, b, :].rearrange("p (c s) -> p c s", c=2), ACT.Copy).then_inc(xt_hi, 2)
            act.activation(Yh[:], Y["low"][:], ACT.Copy).then_inc(rows_hi, 1)
            act.wait_ge(ident_ready, 1)
            act.activation(identr[:], ident[:], ACT.Copy).then_inc(rows_hi, 1)
            split_to(U_MOE + 4)
            act.wait_ge(r_top, 1)
            act.activation(gl[:, 2, :, 0:1], gl[:, 2, :, 0:1], ACT.Exp).then_inc(r_exp, 1)

            def permt(n, pr):
                act.wait_ge(permt_ps, lin(n + 1, pr, 2))
                act.activation(PTr[:, n % 2, :], ps[:, 3, 0:S], ACT.Copy).then_inc(permt_ready, 1)

            def gathered(n, pr):
                for b in range(2):
                    act.wait_ge(gather_ps, lin(2 * n + b + 1, pr, 4))
                    act.activation(xh[:, 4 * b:4 * b + 4, (n % 2) * SLOTS:(n % 2 + 1) * SLOTS],
                                   ps[:, 6 + b, :].rearrange("p (c s) -> p c s", c=4), ACT.Copy).then_inc(gather_hi, 1)

            def expert_step(g, v, d, between=None):
                k = kinds["moe"]
                act.wait_ge(k["ps"], lin(g + 1, d, 2))
                act.activation(SGm[:], ps[:, g % 2, 0:STEP], ACT.Silu).then_inc(k["silu"], 1)
                split(v + 4, d)
                act.wait_ge(k["t"], lin(g + 1, d, 2))
                act.activation(th[:, g % 2, :, :], ps[:, 2, 0:2 * SLOTS].rearrange("p (f s) -> p f s", f=2),
                               ACT.Copy).then_inc(k["hi"], 1)
                if between:
                    between()
                split(v + 5, d)
                split(v + 6, d)

            permt(0, None)
            gathered(0, None)
            with act.Fori(0, E // 2) as pr:
                for b in range(2):
                    u, g, outer = U_MOE + b * FFN_UNITS, b * NSTEP, pr * NSTEP
                    expert_step(g, u, outer)
                    for q in (1, 2):
                        expert_step(g + q, u + 3 * q, outer)
                    with act.Fori(1, DOUBLE - 1) as j:
                        for q in (1, 2):
                            expert_step(g + q, u + 3 * q, outer + j)
                    expert_step(g + NSTEP - 2, u + 3 * (NSTEP - 2), outer)
                    permt(b + 1, pr)
                    expert_step(g + NSTEP - 1, u + 3 * (NSTEP - 1), outer, lambda: gathered(b + 1, pr))
                    act.wait_ge(y_ps, lin(b + 1, pr, 2))
                    act.activation(yh[:], ps[:, 4:6, :].rearrange("p b c -> p (b c)"), ACT.Copy).then_inc(y_hi, 1)

            act.wait_ge(over_ready, 1)
            n_over = act.value_load(over[0:1, 0:1], min_val=0, max_val=OVER)
            with act.If(n_over > 0):
                with act.Fori(0, n_over) as m:
                    expert = act.value_load(over[0:1, bass.ds(m + 1, 1)], min_val=0, max_val=E - 1)
                    act.wait_ge(ov["permt"], m + 1)
                    act.activation(PTo[:], ps[:, 3, 0:S], ACT.Copy).then_inc(ov["pt"], 1)
                    act.wait_ge(ov["gather"], m + 1)
                    act.activation(xo[:], ps[:, 6:8, :].rearrange("p b (c s) -> p (b c) s", c=4), ACT.Copy).then_inc(ov["x"], 1)

                    def chunk(at, k, first=False):
                        rows_g = bass.ds(expert * D, D)
                        if first:
                            act.wait_ge(comb_add, 2 * E + 2)
                            act.wait_ge(ov["x"], m + 1)
                        else:
                            act.wait_ge(ov["down"], k)
                        for dst, w in ((wA, moe_gate), (wB, moe_up)):
                            act.dma_start(dst.rearrange("p (k c) -> p k c", k=KC),
                                          w[rows_g, at].rearrange("(k p) c -> p k c", p=P)).then_inc(ov["gu_in"], 16)
                        act.wait_ge(ov["gu"], k + 1)
                        act.activation(SGo[:], ps[:, 0, 0:P], ACT.Silu).then_inc(ov["silu"], 1)
                        return k

                    def chunk_down(k, row):
                        act.dma_start(wA, moe_down[row, :]).then_inc(ov["down_in"], 16)
                        act.wait_ge(ov["t"], k + 1)
                        act.activation(to[:], ps[:, 2, 0:SLOTS], ACT.Copy).then_inc(ov["h"], 1)

                    chunk(slice(0, P), m * FC, first=True)
                    chunk_down(m * FC, bass.ds(expert * F, P))
                    with act.Fori(1, FC) as i:
                        k = m * FC + i
                        chunk(bass.ds(i * P, P), k)
                        chunk_down(k, bass.ds(expert * F + i * P, P))
                    act.wait_ge(ov["add"], m * 2 + 2)
            act.nop()
            done[0] = U_POOL + 4

            square("low")
            square("low")
            act.wait_ge(pads, 2)
            for c in range(KC):
                act.wait_ge(xt_ps, 4 * 4 + c // 2 + 1)
                ins = act.activation(HF[:, c, MAXW:MAXW + S], ps[:, c // 2, (c % 2) * S:(c % 2 + 1) * S], ACT.Copy,
                                     scale=V[:, COL["norm_mix_2"] + c:COL["norm_mix_2"] + c + 1])
            ins.then_inc(hf_ready, 1)
            vector_load(3, 3)
            vector_load(4, 3)
            act.wait_ge(po_ready, 1)
            act.activation(xh[:], PO[:], ACT.Copy).then_inc(z_ready, 1)
            square("low")
            norm_hi(5, COL["norm_ffn_2"], xh)
            straight_ffn(step_cglu, U_FFN2A, 0)
            vector_load(5, 4)
            act.dma_start(bv2, a["attn_b_qkv_2"][0:1, D + 256:D + 512].to_broadcast([P, 256])).then_inc(bc_in, 16)

            square("low")
            norm_hi(6, COL["norm_mix_2"] + KC, xh)
            split_to(U_Q2 + 6)
            take_qk(2, qT, bias=COL["attn_b_qkv_2"])
            split_to(U_Q2 + 10)
            act.wait_ge(qk_ps, 4)
            for kv in range(KVH):
                col = COL["attn_b_qkv_2"] + KC + kv // 2
                r = 64 * (kv % 2)
                for half in range(2):
                    ins = act.activation(kT2[64 * half:64 * half + 64, kv, :], ps[r:r + 64, 4, (kv // 2) * S:(kv // 2 + 1) * S],
                                         ACT.Identity, bias=V[r:r + 64, col:col + 1])
            ins.then_inc(qk_out, 1)
            split_to(U_WO2 + 6)
            attention(8, 1)
            square("low")
            norm_hi(7, COL["norm_ffn_2"] + KC, xh)
            straight_ffn(step_cglu, U_FFN2B, NSTEP, last=U_END)
            square("low")

        @block.vector
        def _(dve):
            n = [0]
            done = [0]
            norms = [0]
            sums = [0]
            lows = [0]

            def link(ins):
                n[0] += 1
                ins.then_inc(dve_chain, 1)
                dve.wait_ge(dve_chain, n[0])

            def split(u, d=None):
                s = u % RING
                dve.wait_ge(hi_done, lin(u + 1, d, 6))
                dve.tensor_tensor(wlo[:, s, :], raw[:, s, :], whi[:, s, :].bitcast(F32), ALU.subtract).then_inc(lo_done, 1)

            def split_to(u):
                for v in range(done[0], min(u, U_END)):
                    split(v)
                done[0] = max(done[0], u)

            def rsqrt(r, v, t):
                link(dve.tensor_scalar(t.bitcast(U32), v.bitcast(U32), 1, None, ALU.logical_shift_right))
                link(dve.tensor_scalar(r.bitcast(I32), t.bitcast(I32), -1.0, float(0x5F3759DF), ALU.mult, ALU.add))
                for _ in range(3):
                    link(dve.tensor_tensor(t, r, r, ALU.mult))
                    link(dve.scalar_tensor_tensor(t, t, -0.5, v, ALU.mult, ALU.mult))
                    link(dve.scalar_tensor_tensor(r, t, 1.5, r, ALU.add, ALU.mult))

            def rms(where, shared=True):
                for t in range(1 if shared else 0, T):
                    link(dve.tensor_tensor_reduce(junk[where][:], X[:, t, :], X[:, t, :], 1.0, 0.0, ALU.mult, ALU.add,
                                                  st[:, t:t + 1]))
                if shared:
                    sums[0] += 1
                    dve.wait_ge(squares, sums[0])
                link(dve.tensor_scalar(st[:, 2:4], st[:, 0:2], 1.0 / D, EPS, ALU.mult, ALU.add))
                rsqrt(st[:, 4:6], st[:, 2:4], st[:, 6:8])

            def norm(where, shared=True):
                rms(where, shared)
                for t in range(T):
                    ins = dve.tensor_scalar(Y[where][:, t, :], X[:, t, :], st[:, 4 + t:5 + t], None, ALU.mult)
                ins.then_inc(y_ready, 1)
                norms[0] += 1

            def norm_lo(gain, src_hi, dst):
                for c in range(KC):
                    dve.wait_ge(xt_hi, KC * lows[0] + c // 2 * 2 + 2)
                    dve.scalar_tensor_tensor(dst[:, c, :], ps[:, c // 2, (c % 2) * S:(c % 2 + 1) * S],
                                             V[:, gain + c:gain + c + 1], src_hi[:, c, :].bitcast(F32),
                                             ALU.mult, ALU.subtract).then_inc(xt_lo, 1)
                lows[0] += 1

            def acc(t):
                return ps[:, 4 + 2 * t:6 + 2 * t, :].rearrange("p b c -> p (b c)")

            def add_acc(k):
                dve.wait_ge(acc_ps, k + 1)
                for t in range(T):
                    dve.tensor_tensor(X[:, t, :], acc(t), X[:, t, :], ALU.add).then_inc((x_final, acc_free)[t], 1)
                dve.wait_ge(acc_free, k + 1)

            def ahead(v, d, last):
                if last is None or v < last:
                    split(v, d)

            def step_glu(g, s, v, d, j, last):
                k = kinds["glu"]
                p = g % 2
                dve.wait_ge(k["silu"], lin(g + 1, d, 2))
                if g:
                    dve.wait_ge(k["lo"], lin(g, d, 2))
                dve.tensor_tensor(Ht[:], SG[:], ps[:, 2 * p + 1, :].rearrange("p (f s) -> p f s", f=2),
                                  ALU.mult).then_inc(k["mul"], 1)
                ahead(v + 4, d, last)
                dve.wait_ge(k["hi"], lin(g + 1, d, 2))
                dve.tensor_tensor(hl[:, p, :, :], Ht[:], hh[:, p, :, :].bitcast(F32), ALU.subtract).then_inc(k["lo"], 1)
                ahead(v + 5, d, last)
                ahead(v + 6, d, last)

            def step_cglu(g, s, v, d, j, last):
                k = kinds["cglu"]
                p = g % 2
                layer = g // NSTEP
                dve.wait_ge(k["copy"], lin(g + 1, d, 2))
                if g:
                    dve.wait_ge(k["mul"], lin(g, d, 2))
                for tap in (2, 1, 0):
                    for f in range(4):
                        chunk = 2 * s + f % 2 + (F // P) * (f // 2)
                        at = COL["ffn_conv_w_2"] + (layer * CTAPS + tap) * 44 + chunk
                        w = V[:, at:at + 1] if j is None else V[:, bass.ds(j * 4 + at, 1)]
                        op = (2 - tap) * 4 + f
                        if tap == 2:
                            at = COL["ffn_conv_b_2"] + layer * 44 + chunk
                            b = V[:, at:at + 1] if j is None else V[:, bass.ds(j * 4 + at, 1)]
                            ins = dve.tensor_scalar(C2[:, f, :], U2[:, f, 2:2 + S], w, b, ALU.mult, ALU.add)
                        else:
                            dve.wait_ge(k["tap"], lin(12 * g + op - 3, d, 24))
                            ins = dve.scalar_tensor_tensor(C2[:, f, :], U2[:, f, tap:tap + S], w, C2[:, f, :],
                                                           ALU.mult, ALU.add)
                        ins.then_inc(k["tap"], 1)
                dve.wait_ge(k["tap"], lin(12 * g + 12, d, 24))
                dve.sem_inc(k["conv"], 1)
                ahead(v + 4, d, last)
                dve.wait_ge(k["silu"], lin(g + 1, d, 2))
                if g:
                    dve.wait_ge(k["lo"], lin(g, d, 2))
                dve.tensor_tensor(Ht[:], SG[:], C2[:, 0:2, :], ALU.mult).then_inc(k["mul"], 1)
                ahead(v + 5, d, last)
                dve.wait_ge(k["hi"], lin(g + 1, d, 2))
                dve.tensor_tensor(hl[:, p, :, :], Ht[:], hh[:, p, :, :].bitcast(F32), ALU.subtract).then_inc(k["lo"], 1)
                ahead(v + 6, d, last)

            def ffn(step, u, g, outer=None, last=None):
                step(g, 0, u, outer, None, last)
                with dve.Fori(0, DOUBLE - (last is not None)) as j:
                    d = j if outer is None else outer + j
                    step(g + 1, 1, u + 3, d, j, last)
                    step(g + 2, 2, u + 6, d, j, last)
                if last is not None:
                    q = DOUBLE - 1
                    step(g + 1 + 2 * q, 1 + 2 * q, u + 3 + 6 * q, None, None, last)
                    step(g + 2 + 2 * q, 2 + 2 * q, u + 6 + 6 * q, None, None, last)

            def straight_ffn(step, u, g, last=None):
                split_to(u + 4)
                ffn(step, u, g, None, last)
                done[0] = min(u + FFN_UNITS + 4, U_END)

            dve.wait_ge(x_in, 16)
            norm("low", shared=False)
            split_to(2)
            dve.wait_ge(vec_ready, 1)
            norm_lo(COL["mix_norm"], xh, xl)
            dve.memset(U[:, :, 0:PAD], 0.0).then_inc(pads, 1)
            split_to(6)
            dve.wait_ge(bc_in, 32)
            for t in range(T):
                ins = dve.tensor_tensor(X[:, t, :], X[:, t, :], bc[:, 0, :], ALU.add)
            ins.then_inc(bc_free, 1)
            dve.wait_ge(consts_ready, 1)
            dve.tensor_reduce(rows[:], ind[:], AX_X, ALU.add)
            dve.wait_ge(pads, 1)

            def add_products(j):
                dve.wait_ge(tap_done, 2 * V_TAPS * (j + 1))
                dve.wait_ge(conv_ps, j + 1)
                dve.tensor_tensor(C[:, 2 * j:2 * j + 2, :], C[:, 2 * j:2 * j + 2, :],
                                  ps[:, 4 + j, :].rearrange("p (f s) -> p f s", f=2), ALU.add).then_inc(conv_done, 1)

            for j in range(4):
                dve.wait_ge(cin_sig, j + 1)
                for f in range(2):
                    c = 2 * j + f
                    col = COL["conv_b_in"] + c
                    ins = dve.scalar_tensor_tensor(U[:, c, PAD:PAD + S], ps[:, 2 * (j % 2), f * S:(f + 1) * S], V[:, col:col + 1],
                                                   SGc[:, f, :], ALU.add, ALU.mult)
                ins.then_inc(cin_mul, 1)
                dve.wait_ge(cin_mul, j + 1)
                base = 2 * V_TAPS * j
                for f in range(2):
                    c = 2 * j + f
                    w, b = COL["conv_w_dw"] + c, COL["conv_b_dw"] + c
                    dve.tensor_scalar(C[:, c, :], U[:, c, 0:S], V[:, w:w + 1], V[:, b:b + 1], ALU.mult, ALU.add).then_inc(tap_done, 1)
                def further_tap(tap, at, w, f):
                    c = 2 * j + f
                    dve.wait_ge(tap_done, tap)
                    dve.scalar_tensor_tensor(C[:, c, :], U[:, c, at], V[:, w], C[:, c, :], ALU.mult, ALU.add).then_inc(tap_done, 1)

                for f in range(2):
                    w = COL["conv_w_dw"] + KC + 2 * j + f
                    further_tap(base + f + 1, slice(1, 1 + S), slice(w, w + 1), f)
                with dve.Fori(0, V_TURNS) as i:
                    for q in range(4):
                        for f in range(2):
                            further_tap(i * 8 + (base + 2 * (q + 1) + f + 1), bass.ds(i * 4 + (q + 2), S),
                                        bass.ds(i * (4 * KC) + (COL["conv_w_dw"] + (q + 2) * KC + 2 * j + f), 1), f)
                split_to(2 * j + 8)
                if j >= 1:
                    add_products(j - 1)
            add_products(3)

            def every(v, k=KC):
                return v.unsqueeze(1).to_broadcast([P, k, S])

            dve.wait_ge(stat_ps, 1)
            dve.wait_ge(conv_done, 4)
            link(dve.tensor_scalar(MU[:], ps[:, 0, 0:S], 1.0 / D, None, ALU.mult))
            dve.tensor_tensor(C[:], C[:], every(MU), ALU.subtract).then_inc(centered, 1)
            dve.wait_ge(stat_ps, 2)
            link(dve.tensor_scalar(VAR, ps[:, 1, 0:S], 1.0 / D, EPS, ALU.mult, ALU.add))
            rsqrt(RS, VAR, MU)
            dve.wait_ge(centered, 1)
            dve.tensor_tensor(C[:], C[:], every(RS), ALU.mult).then_inc(scaled, 1)
            dve.wait_ge(z_ready, 1)
            dve.tensor_tensor(xl[:], Z[:], xh[:].bitcast(F32), ALU.subtract).then_inc(z_lo, 1)
            dve.wait_ge(small_hi, 2)
            dve.tensor_tensor(wf[:, 1, :, :], wf_raw[:], wf[:, 0, :, :].bitcast(F32), ALU.subtract)
            dve.tensor_tensor(wr[:, 1, :, :], wr_raw[:], wr[:, 0, :, :].bitcast(F32), ALU.subtract)
            dve.tensor_scalar(sink8[:], sink[:], HD ** 0.5, None, ALU.mult).then_inc(small_lo, 1)
            add_acc(0)

            norm("low")
            norm_lo(COL["ffn_norm"], xh, xl)
            straight_ffn(step_glu, U_FFN1, 0)
            add_acc(1)

            norm("high")
            norm_lo(COL["kv_norm"], hnh, hnl)
            norm_lo(COL["mix_norm"] + KC, xh, xl)
            split_to(U_K + 6)
            dve.wait_ge(f_ps, 1)
            link(dve.tensor_tensor(fz[:, 0, :, :], ps[:, 4, 0:T * H].rearrange("p (t h) -> p t h", t=T),
                                   bf[:].unsqueeze(1).to_broadcast([P, T, H]), ALU.add))
            dve.scalar_tensor_tensor(fz[:, 1, :, :], fz[:, 0, :, :], -1.0, fz[:, 0, :, :], ALU.mult, ALU.max).then_inc(f_z, 1)
            dve.tensor_scalar(fz[:, 3, :, :], fz[:, 0, :, :], 0.0, None, ALU.min)
            split_to(U_V + 6)
            link(dve.memset(Lc[:], 0.0))
            dve.wait_ge(f_ln, 1)
            link(dve.tensor_tensor(fz[:, 3, :, :], fz[:, 3, :, :], fz[:, 2, :, :], ALU.subtract))
            for half in range(2):
                for which, s in ((0, HD ** 0.5), (1, -(HD ** 0.5))):
                    at = 64 * half + 16 * which
                    ins = dve.tensor_scalar(Lc[:, :, at:at + H], fz[:, 3, :, :], s, None, ALU.mult)
            ins.then_inc(cum_in, 1)
            dve.wait_ge(acc_ps, 3)
            for t in range(T):
                ins = dve.tensor_copy(vt[:, t, :], acc(t))
            ins.then_inc(acc_free, 1)
            split_to(U_Q + 6)
            dve.wait_ge(cum_ps, 1)
            dve.tensor_scalar(Mq[:], ps[:, 4, 0:S], rows[:, 0:1], rows[:, 1:2], ALU.mult, ALU.add)
            dve.tensor_scalar(Mk[:], ps[:, 4, 0:S], rows[:, 1:2], rows[:, 0:1], ALU.mult, ALU.add).then_inc(cum_ready, 1)
            dve.wait_ge(cum_ready, 1)
            split_to(U_WO + 6)

            def attention(n0, layer):
                def spread_term(g):
                    if g >= 2:
                        dve.wait_ge(sc_ps, n0 + g - 1)
                    q0 = (g // 4) * P
                    for pr in range(2):
                        pair_ = 2 * (g % 4) + pr
                        ins = dve.tensor_scalar(MH[:, g % 2, pr, :], Mq[:, q0:q0 + P], dsel[:, pair_:pair_ + 1], None, ALU.mult)
                    ins.then_inc(mh_ready, 1)

                def largest(g):
                    G, K, b = n0 + g, P if g < 4 else S, 2 * (g % 2)
                    dve.wait_ge(sc_ps, G + 1)
                    for odd in range(2):
                        src = ps[:, b + odd, 0:2 * K].rearrange("p (h k) -> p h k", h=2)
                        if layer == 0:
                            ins = dve.tensor_tensor(src[:, :, K - P:K], src[:, :, K - P:K],
                                                    mask[:, P:S].unsqueeze(1).to_broadcast([P, 2, P]), ALU.add)
                        else:
                            for i in range(2):
                                slope = 2.0 ** (-8.0 / H * (4 * (g % 4) + 2 * i + odd + 1))
                                ins = dve.scalar_tensor_tensor(src[:, i, :], dist[:, S - K:S], slope * HD ** 0.5,
                                                               src[:, i, :], ALU.mult, ALU.add)
                    link(ins)
                    link(dve.tensor_reduce(rmax[:, g, :].rearrange("p (i o) -> p o i", o=2),
                                           ps[:, b:b + 2, 0:2 * K].rearrange("p o (i k) -> p o i k", i=2), AX_X, ALU.max))
                    if layer == 1:
                        sinks = sink8[:, 4 * (g % 4):4 * (g % 4) + 4]
                        link(dve.tensor_tensor(rmax[:, g, :], rmax[:, g, :], sinks, ALU.max))
                        dve.tensor_tensor(esink[:, g, :], sinks, rmax[:, g, :], ALU.subtract)
                    dve.tensor_scalar(nmax[:, g, :], rmax[:, g, :], -(HD ** -0.5), None, ALU.mult).then_inc(sc_max, 1)

                def lower(g):
                    dve.wait_ge(o_hi, n0 + g + 1)
                    c0, q0 = 2 * (g % 4), (g // 4) * P
                    dve.tensor_tensor(xl[:, c0:c0 + 2, q0:q0 + P], ps[:, 6 + g % 2, 0:2 * P].rearrange("p (c q) -> p c q", c=2),
                                      xh[:, c0:c0 + 2, q0:q0 + P].bitcast(F32), ALU.subtract).then_inc(o_lo, 1)

                if layer == 0:
                    spread_term(0)
                    spread_term(1)
                largest(0)
                for g in range(8):
                    G = n0 + g
                    K = P if g < 4 else S
                    dve.wait_ge(sc_exp, G + 1)
                    if layer == 1:
                        link(dve.tensor_tensor(rsum[:, g, :], rsum[:, g, :], esink[:, g, :], ALU.add))
                    link(dve.reciprocal(rinv[:, g, :], rsum[:, g, :]))
                    dve.tensor_tensor(SC[:, :, 0:K], SC[:, :, 0:K], rinv[:, g, :].unsqueeze(2).to_broadcast([P, 4, K]),
                                      ALU.mult).then_inc(sc_norm, 1)
                    if layer == 0 and g < 6:
                        spread_term(g + 2)
                    if g < 7:
                        largest(g + 1)
                    if g:
                        lower(g - 1)
                    dve.wait_ge(pt_ps, G + 1)
                    if g:
                        dve.wait_ge(o_ps, G)
                    dve.tensor_copy(PT[:, 0, :, :], ps[:, 4, :].rearrange("p (h q) -> p h q", h=4)).then_inc(pt_v, 1)
                lower(7)

            attention(0, 0)
            add_acc(3)

            rms("low")
            dve.wait_ge(bc_in, 48)
            for t in range(T):
                ins = dve.scalar_tensor_tensor(Y["low"][:, t, :], X[:, t, :], st[:, 4 + t:5 + t], bc[:, 0, :], ALU.mult, ALU.mult)
            ins.then_inc(y_ready, 1)
            for b in range(4):
                dve.wait_ge(xt_hi, KC * lows[0] + 2 * b + 2)
                dve.tensor_tensor(xl[:, 2 * b:2 * b + 2, :], ps[:, b, :].rearrange("p (c s) -> p c s", c=2),
                                  xh[:, 2 * b:2 * b + 2, :].bitcast(F32), ALU.subtract).then_inc(xt_lo, 2)
            lows[0] += 1
            dve.wait_ge(rows_hi, 1)
            dve.tensor_tensor(Yl[:], Y["low"][:], Yh[:].bitcast(F32), ALU.subtract).then_inc(rows_lo, 1)
            dve.memset(gate[:], 0.0)
            dve.memset(rank[:], 0.0)
            dve.memset(yh[:].bitcast(F32), 0.0)
            dve.memset(yl[:].bitcast(F32), 0.0)
            dve.memset(PTr[:].bitcast(F32), 0.0).then_inc(y_lo, 1)
            split_to(U_MOE + 4)
            dve.wait_ge(y_lo, 1)
            dve.wait_ge(r_ps, 1)
            parts = ps[:, 4, 0:2 * T * E].rearrange("p (t h e) -> p t h e", t=T, h=2)
            link(dve.tensor_tensor(gl[:, 0, :, :], parts[:, :, 0, :], rb[:].unsqueeze(1).to_broadcast([P, T, E]), ALU.add))
            link(dve.tensor_tensor(gl[:, 0, :, :], parts[:, :, 1, :], gl[:, 0, :, :], ALU.add))
            for t in range(T):
                link(dve.max(gl[:, 1, t, :], gl[:, 0, t, :]))
                link(dve.max_index(gi[:, t, :], gl[:, 1, t, :], gl[:, 0, t, :]))
            link(dve.tensor_copy(gl[:, 3, :, :], gi[:]))
            dve.tensor_tensor(gl[:, 2, :, 0:1], gl[:, 1, :, 1:2], gl[:, 1, :, 0:1], ALU.subtract).then_inc(r_top, 1)
            sel = rt[:, 0:2, :]
            for t in range(T):
                dve.tensor_scalar(sel[:, t, :], iota8[:], gl[:, 3, t, 0:1], None, ALU.is_equal)
                link(dve.tensor_scalar(rt[:, 2 + t, :], iota8[:], gl[:, 3, t, 1:2], None, ALU.is_equal))
            dve.tensor_tensor(sel, sel, rt[:, 2:4, :], ALU.add).then_inc(sel_ready, 1)
            dve.wait_ge(r_exp, 1)
            link(dve.tensor_scalar(gl[:, 2, :, 1:2], gl[:, 2, :, 0:1], 1.0, None, ALU.add))
            link(dve.reciprocal(gl[:, 2, :, 2:3], gl[:, 2, :, 1:2]))
            link(dve.tensor_tensor(gl[:, 2, :, 3:4], gl[:, 2, :, 0:1], gl[:, 2, :, 2:3], ALU.mult))
            for t in range(T):
                dve.tensor_scalar(gate[:, t, 1:E + 1], iota8[:], gl[:, 3, t, 0:1], gl[:, 2, t, 2:3], ALU.is_equal, ALU.mult)
                link(dve.tensor_scalar(gl[:, 0, t, :], iota8[:], gl[:, 3, t, 1:2], gl[:, 2, t, 3:4], ALU.is_equal, ALU.mult))
            link(dve.tensor_tensor(gate[:, :, 1:E + 1], gate[:, :, 1:E + 1], gl[:, 0, :, :], ALU.add))
            dve.wait_ge(rank_ps, 1)
            dve.wait_ge(sel_ready, 1)
            link(dve.tensor_tensor(rank[:, :, 1:E + 1], ps[:, 5, 0:T * E].rearrange("p (t e) -> p t e", t=T), sel, ALU.mult))
            dve.wait_ge(consts_ready, 2)

            def perm(n, pr):
                if pr is not None:
                    dve.wait_ge(gather_ps, lin(2 * n, pr, 4))
                for t in range(T):
                    col = rank[:, t, n + 1:n + 2] if pr is None else rank[:, t, bass.ds(pr * 2 + (n + 1), 1)]
                    ins = dve.tensor_scalar(Pm[:, t, :], order[:, 0:SLOTS], col, None, ALU.is_equal)
                ins.then_inc(perm_ready, 1)

            def gathered(n, pr):
                for b in range(2):
                    half = slice((n % 2) * SLOTS, (n % 2 + 1) * SLOTS)
                    dve.wait_ge(gather_hi, lin(2 * n + b + 1, pr, 4))
                    dve.tensor_tensor(xl[:, 4 * b:4 * b + 4, half], ps[:, 6 + b, :].rearrange("p (c s) -> p c s", c=4),
                                      xh[:, 4 * b:4 * b + 4, half].bitcast(F32), ALU.subtract).then_inc(gather_lo, 1)

            def combined(n, t, pr):
                dve.wait_ge(comb_ps, lin(2 * n + t + 1, pr, 4))
                col = gate[:, t, n:n + 1] if pr is None else gate[:, t, bass.ds(pr * 2 + n, 1)]
                dve.scalar_tensor_tensor(X[:, t, :], ps[:, 6:8, :].rearrange("p b c -> p (b c)"), col, X[:, t, :],
                                         ALU.mult, ALU.add).then_inc(comb_add, 1)
                dve.wait_ge(comb_add, lin(2 * n + t + 1, pr, 4))

            perm(0, None)
            link(dve.memset(rt[:, 4:16, :], 0.0))
            more = rt[:, 4, :]
            link(dve.tensor_scalar(more, ps[:, 5, T * E:(T + 1) * E], float(SLOTS), None, ALU.is_gt))
            pads_ = [rt[:, 6:8, :].rearrange("p a b -> p (a b)"), rt[:, 8:10, :].rearrange("p a b -> p (a b)")]
            link(dve.tensor_copy(pads_[0][:, 8:16], more))
            for i, w in enumerate((1, 2, 4)):
                src, dst = pads_[i % 2], pads_[(i + 1) % 2]
                link(dve.tensor_tensor(dst[:, 8:16], src[:, 8:16], src[:, 8 - w:16 - w], ALU.add))
            upto = pads_[1]
            link(dve.tensor_copy(rt[:, 10, 0:1], upto[:, 15:16]))
            for m in range(OVER):
                hot = rt[:, 12 + m, :]
                link(dve.scalar_tensor_tensor(hot, upto[:, 8:16], float(m + 1), more, ALU.is_equal, ALU.mult))
                link(dve.tensor_tensor_reduce(rt[:, 11, :], hot, iota8[:], 1.0, 0.0, ALU.mult, ALU.add, rt[:, 10, m + 1:m + 2]))
                for t in range(T):
                    link(dve.tensor_tensor_reduce(rt[:, 11, :], hot, rank[:, t, 1:E + 1], 1.0, 0.0, ALU.mult, ALU.add,
                                                  rank_o[:, t, m:m + 1]))
                    link(dve.tensor_tensor_reduce(rt[:, 11, :], hot, gate[:, t, 1:E + 1], 1.0, 0.0, ALU.mult, ALU.add,
                                                  gate_o[:, t, m:m + 1]))
            dve.tensor_copy(over[:], rt[:, 10, 0:1 + OVER]).then_inc(over_ready, 1)
            gathered(0, None)

            def expert_step(g, v, d, between=None):
                k = kinds["moe"]
                dve.wait_ge(k["silu"], lin(g + 1, d, 2))
                dve.tensor_tensor(Hm[:], SGm[:], ps[:, g % 2, STEP:2 * STEP], ALU.mult).then_inc(k["mul"], 1)
                split(v + 4, d)
                dve.wait_ge(k["hi"], lin(g + 1, d, 2))
                dve.tensor_tensor(tl[:, g % 2, :, :], ps[:, 2, 0:2 * SLOTS].rearrange("p (f s) -> p f s", f=2),
                                  th[:, g % 2, :, :].bitcast(F32), ALU.subtract).then_inc(k["lo"], 1)
                if between:
                    between()
                split(v + 5, d)
                split(v + 6, d)

            with dve.Fori(0, E // 2) as pr:
                for b in range(2):
                    u, g, outer = U_MOE + b * FFN_UNITS, b * NSTEP, pr * NSTEP
                    expert_step(g, u, outer)
                    combined(b, 0, pr)
                    expert_step(g + 1, u + 3, outer)
                    combined(b, 1, pr)
                    expert_step(g + 2, u + 6, outer)
                    perm(b + 1, pr)
                    with dve.Fori(1, DOUBLE - 1) as j:
                        for q in (1, 2):
                            expert_step(g + q, u + 3 * q, outer + j)
                    expert_step(g + NSTEP - 2, u + 3 * (NSTEP - 2), outer)
                    expert_step(g + NSTEP - 1, u + 3 * (NSTEP - 1), outer, lambda: gathered(b + 1, pr))
                    dve.wait_ge(y_hi, lin(b + 1, pr, 2))
                    dve.tensor_tensor(yl[:], ps[:, 4:6, :].rearrange("p b c -> p (b c)"), yh[:].bitcast(F32),
                                      ALU.subtract).then_inc(y_lo, 1)
            for t in range(T):
                combined(E, t, None)
            dve.wait_ge(comb_add, 2 * E + 2)
            done[0] = U_POOL + 4

            n_over = dve.value_load(over[0:1, 0:1], min_val=0, max_val=OVER)
            with dve.If(n_over > 0):
                with dve.Fori(0, n_over) as m:
                    for t in range(T):
                        ins = dve.tensor_scalar(Pm[:, t, :], order[:, SLOTS:2 * SLOTS], rank_o[:, t, bass.ds(m, 1)], None,
                                                ALU.is_equal)
                    ins.then_inc(ov["perm"], 1)
                    with dve.Fori(0, FC) as i:
                        k = m * FC + i
                        dve.wait_ge(ov["silu"], k + 1)
                        dve.tensor_tensor(Ho[:], SGo[:], ps[:, 0, P:2 * P], ALU.mult).then_inc(ov["mul"], 1)
                        dve.wait_ge(ov["down"], k + 1)
                    dve.tensor_copy(yo[:], ps[:, 4:6, :].rearrange("p b c -> p (b c)")).then_inc(ov["y"], 1)
                    for t in range(T):
                        dve.wait_ge(ov["comb"], m * 2 + t + 1)
                        dve.scalar_tensor_tensor(X[:, t, :], ps[:, 6:8, :].rearrange("p b c -> p (b c)"),
                                                 gate_o[:, t, bass.ds(m, 1)], X[:, t, :], ALU.mult, ALU.add).then_inc(ov["add"], 1)
                    dve.wait_ge(ov["add"], m * 2 + 2)
                    dve.nop()
            dve.sem_inc(x_final, 1)
            dve.sem_inc(bc_free, 1)

            rms("low")
            for t in range(T):
                dve.scalar_tensor_tensor(X[:, t, :], X[:, t, :], st[:, 4 + t:5 + t], bc[:, 1, :], ALU.mult,
                                         ALU.mult).then_inc((x_final, bc_free)[t], 1)
            dve.wait_ge(bc_free, 3)

            norm("low")
            dve.wait_ge(consts_ready, 2)
            dve.memset(HF[:, :, 0:MAXW], 0.0).then_inc(pads, 1)
            dve.memset(SA[:, :, 0:MAXW], 0.0)
            dve.memset(SB[:, :, 0:MAXW], 0.0)
            for g, win in enumerate(WINDOWS):
                ins = dve.tensor_scalar(edge[:, g, :], order[:, 0:MAXW], float(win), None, ALU.min)
            link(ins)
            link(dve.reciprocal(edge[:], edge[:]))
            for g, win in enumerate(WINDOWS):
                ins = dve.tensor_scalar(edge[:, g, :], edge[:, g, :], float(win), None, ALU.mult)
            link(ins)
            dve.wait_ge(hf_ready, 1)
            for g, win in enumerate(WINDOWS):
                c = 2 * g
                src = HF[:, c:c + 2, :]
                nxt = [SA, SB]
                width = 1
                while width < win:
                    dst = nxt[0]
                    link(dve.tensor_tensor(dst[:, :, MAXW:], src[:, :, MAXW:], src[:, :, MAXW - width:MAXW + S - width], ALU.add))
                    src, nxt, width = dst, nxt[::-1], 2 * width
                link(dve.tensor_tensor(src[:, :, MAXW:2 * MAXW], src[:, :, MAXW:2 * MAXW],
                                       edge[:, g, :].unsqueeze(1).to_broadcast([P, 2, MAXW]), ALU.mult))
                ins = dve.scalar_tensor_tensor(PO[:, c:c + 2, :], src[:, :, MAXW:], 1.0 / win, HF[:, c:c + 2, MAXW:],
                                               ALU.mult, ALU.subtract)
                link(ins) if g < 3 else ins.then_inc(po_ready, 1)
            dve.wait_ge(z_ready, 2)
            dve.tensor_tensor(xl[:], PO[:], xh[:].bitcast(F32), ALU.subtract).then_inc(z_lo, 1)
            dve.wait_ge(bc_in, 16 * 5)
            link(dve.tensor_tensor(Y["low"][:, 0, :], bc[:, 0, :], bc[:, 1, :], ALU.mult))
            for t in range(T):
                ins = dve.tensor_tensor(X[:, t, :], X[:, t, :], Y["low"][:, 0, :], ALU.add)
            link(ins)
            dve.wait_ge(acc_ps, 5)
            for t in range(T):
                link(dve.tensor_tensor(Y["low"][:, t, :], acc(t), bc[:, 1, :], ALU.mult))
                dve.tensor_tensor(X[:, t, :], X[:, t, :], Y["low"][:, t, :], ALU.add).then_inc((x_final, bc_free)[t], 1)
            dve.wait_ge(bc_free, 4)
            dve.sem_inc(acc_free, 1)

            def conv_ffn(u, layer, k, last=None):
                norm("low")
                norm_lo(COL["norm_ffn_2"] + layer * KC, xh, xl)
                dve.memset(U2[:, :, 0:2], 0.0).then_inc(pads, 1)
                straight_ffn(step_cglu, u, layer * NSTEP, last)
                add_acc(k)

            conv_ffn(U_FFN2A, 0, 5)

            norm("low")
            norm_lo(COL["norm_mix_2"] + KC, xh, xl)
            split_to(U_Q2 + 10)
            dve.wait_ge(qk_ps, 4)
            dve.wait_ge(bc_in, 16 * 7)
            for t in range(T):
                ins = dve.tensor_tensor(vt2[:, t, :], ps[:, 6 + t, 0:256], bv2, ALU.add)
            ins.then_inc(v2_ready, 1)
            split_to(U_WO2 + 6)
            dve.wait_ge(consts_ready, 3)
            attention(8, 1)
            add_acc(6)
            conv_ffn(U_FFN2B, 1, 7, last=U_END)
            rms("low")
            for t in range(T):
                dve.scalar_tensor_tensor(Y["low"][:, t, :], X[:, t, :], st[:, 4 + t:5 + t], bc[:, 0, :], ALU.mult,
                                         ALU.mult).then_inc(y_ready, 1)

        @block.tensor
        def _(pe):
            def norm_t(k, where):
                pe.wait_ge(y_ready, k + 1)
                for c in range(KC):
                    for t in range(T):
                        at = (c % 2) * S + t * P
                        ins = pe.transpose(ps[:, c // 2, at:at + P], Y[where][:, t, c * P:(c + 1) * P], ident[:])
                    if c % 2:
                        ins.then_inc(xt_ps, 1)

            def feat(dst, s, cols, h, l, start, stop=False):
                pe.matmul(dst, whi[:, s, cols], h, start=start, stop=False, skip_group_check=True)
                pe.matmul(dst, whi[:, s, cols], l, start=False, stop=False, skip_group_check=True)
                return pe.matmul(dst, wlo[:, s, cols], h, start=False, stop=stop, skip_group_check=True)

            def toks(dst, s, cols, h, l, start, stop):
                pe.matmul(dst, h, whi[:, s, cols], start=start, stop=False, skip_group_check=True)
                pe.matmul(dst, l, whi[:, s, cols], start=False, stop=False, skip_group_check=True)
                return pe.matmul(dst, h, wlo[:, s, cols], start=False, stop=stop, skip_group_check=True)

            def split_in(u, d=None):
                pe.wait_ge(lo_done, lin(u + 1, d, 6))

            def gate_up(u, p, d):
                for kh in range(2):
                    split_in(u + kh, d)
                    s = (u + kh) % RING
                    for f in range(4):
                        for k in range(4):
                            kk = 4 * kh + k
                            c0 = k * 2 * STEP + f * P
                            ins = feat(ps[:, 2 * p + f // 2, (f % 2) * S:(f % 2 + 1) * S], s, slice(c0, c0 + P),
                                       xh[:, kk, :], xl[:, kk, :], start=(kk == 0 and f % 2 == 0), stop=(kk == KC - 1))
                    ins.then_inc(unit_used, 1)
                return ins

            def token_major(k, u, n=4, after=None, h=xh, l=xl):
                pe.wait_ge(acc_free, k)
                for i in range(n):
                    split_in(u + i)
                    s = (u + i) % RING
                    for kk in range(2):
                        c = 2 * i + kk
                        for t in range(T):
                            for half in range(2):
                                c0 = kk * D + half * 512
                                ins = toks(ps[:, 4 + 2 * t + half, :], s, slice(c0, c0 + 512), h[:, c, t * P:(t + 1) * P],
                                           l[:, c, t * P:(t + 1) * P], start=(c == 0), stop=(c == 2 * n - 1))
                    ins.then_inc(unit_used, 1)
                pe.wait_ge(unit_used, u + n)
                pe.sem_inc(acc_ps, 1)

            def feat_major(i, u, h=xh, l=xl):
                for q in range(4):
                    split_in(u + q)
                    s = (u + q) % RING
                    for kk in range(2):
                        k = 2 * q + kk
                        for c in range(KC):
                            c0 = kk * D + c * P
                            ins = feat(ps[:, c // 2, (c % 2) * S:(c % 2 + 1) * S], s, slice(c0, c0 + P), h[:, k, :], l[:, k, :],
                                       start=(k == 0 and c % 2 == 0), stop=(k == KC - 1))
                    ins.then_inc(unit_used, 1)
                pe.wait_ge(unit_used, u + 4)
                pe.sem_inc(qk_ps, 1)

            def down(k, g, u, d, first=False):
                pe.wait_ge(k["lo"], lin(g + 1, d, 2))
                split_in(u, d)
                s = u % RING
                p = g % 2
                for f in range(2):
                    for t in range(T):
                        for half in range(2):
                            c0 = f * D + half * 512
                            ins = toks(ps[:, 4 + 2 * t + half, :], s, slice(c0, c0 + 512), hh[:, p, f, t * P:(t + 1) * P],
                                       hl[:, p, f, t * P:(t + 1) * P], start=(first and f == 0), stop=False)
                ins.then_inc(unit_used, 1)

            def ffn(kind, u, g, k, outer=None, kd=None):
                sems = kinds[kind]
                read = sems["mul"] if kind == "glu" else sems["copy"]

                def up(g, u, d):
                    if d is not None or g >= 2:
                        pe.wait_ge(read, lin(g - 1, d, 2))
                    gate_up(u, g % 2, d)
                    pe.wait_ge(unit_used, lin(u + 2, d, 6))
                    pe.sem_inc(sems["ps"], 1)

                def double(g, u, d, first=False):
                    up(g, u, d)
                    if first:
                        pe.wait_ge(acc_free, k if kd is None else kd * 2 + k)
                    down(sems, g - 1, u + 2, d, first)
                    up(g + 1, u + 3, d)
                    down(sems, g, u + 5, d)

                up(g, u, outer)
                double(g + 1, u + 2, outer, first=True)
                with pe.Fori(1, DOUBLE) as j:
                    double(g + 1, u + 2, j if outer is None else outer + j)
                down(sems, g + NSTEP - 1, u + FFN_UNITS - 1, outer)
                pe.wait_ge(unit_used, lin(u + FFN_UNITS, outer, 6))
                pe.sem_inc(acc_ps, 1)

            def normed(evac):
                pe.wait_ge(xt_lo, KC * (evac + 1))

            pe.wait_ge(ident_ready, 1)
            pe.wait_ge(vec_in, 16 * len(vector_rows()))
            for b in range(NBLK):
                m = min(P, NCOL - b * P)
                ins = pe.transpose(ps[:, 6 + b // 4, (b % 4) * P:(b % 4) * P + m], stage[0:m, b, :], ident[0:m, 0:m])
            ins.then_inc(vec_ps, 1)

            def taps(j):
                pe.wait_ge(cin_mul, j + 1)
                base = 2 * PE_TAPS * j

                def one(slot, n, at, f, start=False, stop=False):
                    pe.wait_ge(diag_ready, n + 1)
                    return pe.matmul(ps[:, 4 + j, f * S:(f + 1) * S], diag[:, slot, :], U[:, 2 * j + f, at], start=start,
                                     stop=stop, skip_group_check=True).then_inc(diag_free, 1)

                for f in range(2):
                    one(DIAGS + f, base + f, slice(V_TAPS, V_TAPS + S), f, start=(f == 0))
                with pe.Fori(0, PE_TURNS) as i:
                    for m in range(DIAGS):
                        one(m, i * DIAGS + (base + 2 + m), bass.ds(i * (DIAGS // 2) + (V_TAPS + 1 + m // 2), S), m % 2)
                pe.wait_ge(diag_free, DIAGS + 2 + base + 2 * PE_TAPS)
                pe.sem_inc(conv_ps, 1)

            norm_t(0, "low")
            normed(0)
            for j in range(4):
                if j >= 2:
                    pe.wait_ge(cin_mul, j - 1)
                gate_up(U_CONV_IN + 2 * j, j % 2, None)
                pe.wait_ge(unit_used, 2 * j + 2)
                pe.sem_inc(cin_ps, 1)
                if j >= 1:
                    taps(j - 1)
            taps(3)
            pe.wait_ge(consts_ready, 1)
            for c in range(KC):
                pe.wait_ge(conv_done, c // 2 + 1)
                ins = pe.matmul(ps[:, 0, 0:S], ones[:], C[:, c, :], start=(c == 0), stop=(c == KC - 1))
            ins.then_inc(stat_ps, 1)
            pe.wait_ge(squared, 1)
            for c in range(KC):
                ins = pe.matmul(ps[:, 1, 0:S], ones[:], Z[:, c, :], start=(c == 0), stop=(c == KC - 1))
            ins.then_inc(stat_ps, 1)
            pe.wait_ge(z_lo, 1)
            token_major(0, U_CONV_OUT)

            norm_t(1, "low")
            normed(1)
            ffn("glu", U_FFN1, 0, 1)

            norm_t(2, "high")
            normed(3)
            feat_major(0, U_K, hnh, hnl)
            pe.wait_ge(small_lo, 1)
            for t in range(T):
                dst = ps[:, 4, t * H:(t + 1) * H]
                for c in range(KC):
                    h_, l_ = hnh[:, c, t * P:(t + 1) * P], hnl[:, c, t * P:(t + 1) * P]
                    pe.matmul(dst, h_, wf[:, 0, c, :], start=(c == 0), stop=False)
                    pe.matmul(dst, l_, wf[:, 0, c, :], start=False, stop=False)
                    ins = pe.matmul(dst, h_, wf[:, 1, c, :], start=False, stop=(c == KC - 1))
            ins.then_inc(f_ps, 1)
            pe.wait_ge(f_z, 1)
            token_major(2, U_V, h=hnh, l=hnl)
            pe.wait_ge(qk_out, 1)
            feat_major(1, U_Q)
            pe.wait_ge(acc_free, 3)
            pe.wait_ge(cum_in, 1)
            pe.matmul(ps[:, 4, 0:S], Lc[:, 0, :], tri[:], start=True, stop=False)
            pe.matmul(ps[:, 4, P:S], Lc[:, 1, :], tri[:, 0:P], start=False, stop=True).then_inc(cum_ps, 1)

            def attention(n0, layer):
                def scores(g):
                    G = n0 + g
                    K = P if g < 4 else S
                    q0 = (g // 4) * P
                    if g >= 2:
                        pe.wait_ge(sc_max, G - 1)
                    if layer == 0:
                        pe.wait_ge(mh_ready, g + 1)
                    for h in range(4):
                        hd = 4 * (g % 4) + h
                        r = 64 * (h % 2)
                        dst = ps[:, 2 * (g % 2) + h % 2, (h // 2) * K:(h // 2 + 1) * K]
                        keys = kT[r:r + 64, hd // 2, 0:K] if layer == 0 else kT2[r:r + 64, g % 4, 0:K]
                        ins = pe.matmul(dst, qT[r:r + 64, hd // 2, q0:q0 + P], keys, start=True, stop=(layer == 1))
                        if layer == 0:
                            ins = pe.matmul(dst, MH[r:r + 64, g % 2, h // 2, :], Mk[r:r + 64, 0:K], start=False, stop=True)
                    ins.then_inc(sc_ps, 1)

                scores(0)
                scores(1)
                for g in range(8):
                    G = n0 + g
                    nk = 1 if g < 4 else 2
                    pe.wait_ge(sc_norm, G + 1)
                    if g:
                        pe.wait_ge(pt_v, G)
                    for kc in range(nk):
                        for h in range(4):
                            ins = pe.transpose(ps[:, 4 + kc, h * P:(h + 1) * P], SC[:, h, kc * P:(kc + 1) * P], ident[:])
                    ins.then_inc(pt_ps, 1)
                    if g < 6:
                        scores(g + 2)
                    pe.wait_ge(pt_v, G + 1)
                    if g >= 4:
                        pe.wait_ge(pt_a, 4 * layer + g - 3)
                    if g >= 2:
                        pe.wait_ge(o_lo, G - 1)
                    for h in range(4):
                        hd = 4 * (g % 4) + h
                        for kc in range(nk):
                            vals = vt[:, kc, hd * HD:(hd + 1) * HD] if layer == 0 else vt2[:, kc, (g % 4) * HD:(g % 4 + 1) * HD]
                            ins = pe.matmul(ps[64 * (h % 2):64 * (h % 2) + 64, 6 + g % 2, (h // 2) * P:(h // 2 + 1) * P], vals,
                                            PT[:, kc, h, :], start=(kc == 0), stop=(kc == nk - 1))
                    ins.then_inc(o_ps, 1)
                pe.wait_ge(o_lo, n0 + 8)

            pe.wait_ge(qk_out, 2)
            pe.wait_ge(cum_ready, 1)
            attention(0, 0)
            token_major(3, U_WO)

            norm_t(3, "low")
            normed(4)
            for t in range(T):
                dst = ps[:, 4, 2 * t * E:2 * (t + 1) * E]
                for c in range(KC):
                    h_, l_ = xh[:, c, t * P:(t + 1) * P], xl[:, c, t * P:(t + 1) * P]
                    pe.matmul(dst, h_, wr[:, :, c, :], start=(c == 0), stop=False)
                    ins = pe.matmul(dst, l_, wr[:, :, c, :], start=False, stop=(c == KC - 1))
            ins.then_inc(r_ps, 1)
            pe.wait_ge(sel_ready, 1)
            sel = rt[:, 0:2, :]
            pe.matmul(ps[:, 5, 0:E], tri[:, 0:P], sel[:, 0, :], start=True, stop=True)
            pe.matmul(ps[:, 5, E:2 * E], ones[:], sel[:, 0, :], start=True, stop=False)
            pe.matmul(ps[:, 5, E:2 * E], tri[:, 0:P], sel[:, 1, :], start=False, stop=True)
            for t in range(T):
                ins = pe.matmul(ps[:, 5, 2 * E:3 * E], ones[:], sel[:, t, :], start=(t == 0), stop=(t == T - 1))
            ins.then_inc(rank_ps, 1)

            def permt(n, pr):
                pe.wait_ge(perm_ready, lin(n + 1, pr, 2))
                if pr is not None:
                    pe.wait_ge(permt_ready, lin(n, pr, 2))
                for t in range(T):
                    ins = pe.matmul(ps[:, 3, t * P:(t + 1) * P], Pm[:, t, :], identr[:], start=True, stop=True)
                ins.then_inc(permt_ps, 1)

            def gather(n, pr):
                if pr is not None:
                    pe.wait_ge(comb_add, lin(2 * n, pr, 4))
                for c in range(KC):
                    for t in range(T):
                        dst = ps[:, 6 + c // 4, (c % 4) * SLOTS:(c % 4 + 1) * SLOTS]
                        pe.matmul(dst, Yh[:, t, c * P:(c + 1) * P], Pm[:, t, :], start=(t == 0), stop=False)
                        ins = pe.matmul(dst, Yl[:, t, c * P:(c + 1) * P], Pm[:, t, :], start=False, stop=(t == T - 1))
                    if c % 4 == 3:
                        ins.then_inc(gather_ps, 1)

            def combine(n, t, pr):
                pe.wait_ge(gather_lo, lin(2 * n + 2, pr, 4))
                pe.wait_ge(y_lo, lin(n + 1, pr, 2))
                if t:
                    pe.wait_ge(comb_add, lin(2 * n + 1, pr, 4))
                for half in range(2):
                    for i, y in enumerate((yh, yl)):
                        ins = pe.matmul(ps[:, 6 + half, :], PTr[:, (n + 1) % 2, t * P:(t + 1) * P],
                                        y[:, half * 512:(half + 1) * 512], start=(i == 0), stop=(i == 1))
                ins.then_inc(comb_ps, 1)

            moe = kinds["moe"]

            def expert_up(g, u, d, n):
                if g >= 2:
                    pe.wait_ge(moe["mul"], lin(g - 1, d, 2))
                for kh in range(2):
                    split_in(u + kh, d)
                    s = (u + kh) % RING
                    for k in range(4):
                        c = 4 * kh + k
                        half = slice((n % 2) * SLOTS, (n % 2 + 1) * SLOTS)
                        ins = toks(ps[:, g % 2, :], s, slice(k * 512, (k + 1) * 512), xh[:, c, half], xl[:, c, half],
                                   start=(c == 0), stop=(c == KC - 1))
                    ins.then_inc(unit_used, 1)
                pe.wait_ge(unit_used, lin(u + 2, d, 6))
                pe.sem_inc(moe["ps"], 1)

            def turn(g, d):
                pe.wait_ge(moe["mul"], lin(g + 1, d, 2))
                if g:
                    pe.wait_ge(moe["lo"], lin(g, d, 2))
                for f in range(2):
                    ins = pe.transpose(ps[:, 2, f * SLOTS:(f + 1) * SLOTS], Hm[:, f * P:(f + 1) * P], ident[:])
                ins.then_inc(moe["t"], 1)

            def expert_down(g, u, d, first=False, last=False):
                pe.wait_ge(moe["lo"], lin(g + 1, d, 2))
                split_in(u, d)
                s = u % RING
                for f in range(2):
                    for half in range(2):
                        c0 = f * D + half * 512
                        ins = toks(ps[:, 4 + half, :], s, slice(c0, c0 + 512), th[:, g % 2, f, :], tl[:, g % 2, f, :],
                                   start=(first and f == 0), stop=(last and f == 1))
                ins.then_inc(unit_used, 1)

            permt(0, None)
            gather(0, None)
            with pe.Fori(0, E // 2) as pr:
                for b in range(2):
                    u, g, outer = U_MOE + b * FFN_UNITS, b * NSTEP, pr * NSTEP
                    pe.wait_ge(gather_lo, lin(2 * b + 2, pr, 4))
                    expert_up(g, u, outer, b)
                    pe.wait_ge(permt_ready, lin(b + 1, pr, 2))
                    combine(b, 0, pr)
                    turn(g, outer)
                    expert_up(g + 1, u + 2, outer, b)
                    combine(b, 1, pr)
                    expert_down(g, u + 4, outer, first=True)
                    turn(g + 1, outer)
                    expert_up(g + 2, u + 5, outer, b)
                    expert_down(g + 1, u + 7, outer)
                    turn(g + 2, outer)
                    with pe.Fori(1, DOUBLE - 1) as j:
                        d = outer + j
                        for q in (1, 2):
                            expert_up(g + q, u + 3 * q - 1, d, b)
                            expert_down(g + q - 1, u + 3 * q + 1, d)
                            turn(g + q, d)
                    q = NSTEP - 2
                    expert_up(g + q, u + 3 * q - 1, outer, b)
                    expert_down(g + q - 1, u + 3 * q + 1, outer)
                    turn(g + q, outer)
                    permt(b + 1, pr)
                    q = NSTEP - 1
                    expert_up(g + q, u + 3 * q - 1, outer, b)
                    expert_down(g + q - 1, u + 3 * q + 1, outer)
                    turn(g + q, outer)
                    gather(b + 1, pr)
                    expert_down(g + q, u + FFN_UNITS - 1, outer, last=True)
                    pe.wait_ge(unit_used, lin(u + FFN_UNITS, outer, 6))
                    pe.sem_inc(y_ps, 1)
            for t in range(T):
                combine(E, t, None)

            pe.wait_ge(over_ready, 1)
            n_over = pe.value_load(over[0:1, 0:1], min_val=0, max_val=OVER)
            with pe.If(n_over > 0):
                with pe.Fori(0, n_over) as m:
                    pe.wait_ge(ov["perm"], m + 1)
                    pe.wait_ge(comb_add, 2 * E + 2)
                    for t in range(T):
                        ins = pe.matmul(ps[:, 3, t * P:(t + 1) * P], Pm[:, t, :], identr[:], start=True, stop=True)
                    ins.then_inc(ov["permt"], 1)
                    for c in range(KC):
                        for t in range(T):
                            dst = ps[:, 6 + c // 4, (c % 4) * SLOTS:(c % 4 + 1) * SLOTS]
                            pe.matmul(dst, Yh[:, t, c * P:(c + 1) * P], Pm[:, t, :], start=(t == 0), stop=False)
                            ins = pe.matmul(dst, Yl[:, t, c * P:(c + 1) * P], Pm[:, t, :], start=False, stop=(t == T - 1))
                    ins.then_inc(ov["gather"], 1)
                    pe.wait_ge(ov["x"], m + 1)
                    pe.wait_ge(ov["pt"], m + 1)

                    def chunk(k, first):
                        pe.wait_ge(ov["gu_in"], k * 32 + 32)
                        for h, w in ((0, wA), (1, wB)):
                            for c in range(KC):
                                ins = pe.matmul(ps[:, 0, h * P:(h + 1) * P], xo[:, c, :], w[:, c * P:(c + 1) * P],
                                                start=(c == 0), stop=(c == KC - 1))
                        ins.then_inc(ov["gu"], 1)
                        pe.wait_ge(ov["mul"], k + 1)
                        pe.transpose(ps[:, 2, 0:SLOTS], Ho[:], ident[:]).then_inc(ov["t"], 1)
                        pe.wait_ge(ov["h"], k + 1)
                        pe.wait_ge(ov["down_in"], k * 16 + 16)
                        for half in range(2):
                            ins = pe.matmul(ps[:, 4 + half, :], to[:], wA[:, half * 512:(half + 1) * 512], start=first, stop=False,
                                            skip_group_check=True)
                        ins.then_inc(ov["down"], 1)

                    chunk(m * FC, True)
                    with pe.Fori(1, FC) as i:
                        chunk(m * FC + i, False)
                    pe.wait_ge(ov["y"], m + 1)
                    for t in range(T):
                        if t:
                            pe.wait_ge(ov["add"], m * 2 + 1)
                        for half in range(2):
                            ins = pe.matmul(ps[:, 6 + half, :], PTo[:, t * P:(t + 1) * P], yo[:, half * 512:(half + 1) * 512],
                                            start=True, stop=True)
                        ins.then_inc(ov["comb"], 1)
                    pe.wait_ge(ov["add"], m * 2 + 2)
                    pe.nop()

            norm_t(4, "low")
            pe.wait_ge(z_lo, 2)
            pe.wait_ge(acc_free, 4)
            split_in(U_POOL)
            for t in range(T):
                for g in range(4):
                    for k in range(2):
                        c0 = g * 512 + k * 256
                        ins = toks(ps[:, 4 + 2 * t + g // 2, (g % 2) * 256:(g % 2 + 1) * 256], U_POOL % RING, slice(c0, c0 + 256),
                                   xh[:, 2 * g + k, t * P:(t + 1) * P], xl[:, 2 * g + k, t * P:(t + 1) * P],
                                   start=(k == 0), stop=(k == 1))
            ins.then_inc(unit_used, 1)
            pe.wait_ge(unit_used, U_POOL + 1)
            pe.sem_inc(acc_ps, 1)
            norm_t(5, "low")
            normed(5)
            ffn("cglu", U_FFN2A, 0, 5)

            norm_t(6, "low")
            normed(6)
            feat_major(2, U_Q2)
            for kh in range(2):
                split_in(U_KV2 + kh)
                s = (U_KV2 + kh) % RING
                for k in range(4):
                    kk = 4 * kh + k
                    for f in range(2):
                        c0 = k * 512 + f * P
                        feat(ps[:, 4, f * S:(f + 1) * S], s, slice(c0, c0 + P), xh[:, kk, :], xl[:, kk, :],
                             start=(kk == 0 and f == 0), stop=(kk == KC - 1))
                    for t in range(T):
                        ins = toks(ps[:, 6 + t, 0:256], s, slice(k * 512 + 256, k * 512 + 512), xh[:, kk, t * P:(t + 1) * P],
                                   xl[:, kk, t * P:(t + 1) * P], start=(kk == 0), stop=(kk == KC - 1))
                ins.then_inc(unit_used, 1)
            pe.wait_ge(unit_used, U_KV2 + 2)
            pe.sem_inc(qk_ps, 1)
            pe.wait_ge(qk_out, 4)
            pe.wait_ge(v2_ready, 1)
            attention(8, 1)
            token_major(6, U_WO2)
            norm_t(7, "low")
            normed(7)
            ffn("cglu", U_FFN2B, NSTEP, 7)


_INS = ['x', 'mix_norm', 'ffn_norm', 'conv_w_in', 'conv_b_in', 'conv_w_dw', 'conv_b_dw', 'conv_ln_g', 'conv_ln_b',
        'conv_w_out', 'conv_b_out', 'kv_norm', 'w_kvf', 'b_f', 'w_q', 'w_o', 'ffn_w_gate', 'ffn_w_up', 'ffn_w_down',
        'router_w', 'router_b', 'moe_w_gate', 'moe_w_up', 'moe_w_down', 'final_norm', 'pool_w_2', 'pool_b_2',
        'pool_scale_2', 'attn_w_qkv_2', 'attn_b_qkv_2', 'attn_sinks_2', 'attn_w_o_2', 'norm_mix_2', 'norm_ffn_2',
        'ffn_w_in_2', 'ffn_conv_w_2', 'ffn_conv_b_2', 'ffn_w_out_2', 'norm_f_2']


def kernel(**inputs):
    import numpy as _np
    import concourse.bacc as _bacc
    from concourse import mybir as _mybir
    from concourse.bass_utils import run_bass_kernel_spmd as _run

    nc = _bacc.Bacc("TRN2", target_bir_lowering=False, num_devices=1, dynamic_dma_scratch_size=1024)
    arrays, args = {}, {}
    for name in _INS:
        v = _np.ascontiguousarray(inputs[name])
        arrays[f"in_{name}_dram"] = v
        args[name] = nc.dram_tensor(f"in_{name}_dram", v.shape, _mybir.dt.from_np(v.dtype), kind="ExternalInput").ap()
    out = nc.dram_tensor("out_0_dram", (1, S, D), F32, kind="ExternalOutput").ap()
    build(nc, args, out)
    r = _run(nc, [arrays], core_ids=[0])
    return r.results[0]["out_0_dram"]
```
